# Optimizing a Trainium2 kernel written in Bass

```python
import jax, jax.numpy as jnp
from jax import lax
import numpy as np

D_MODEL = 1024
BATCH = 1
SEQ = 1024
DEPTH = 1

N_Q_HEADS = 16
N_KV_HEADS = 4
HEAD_DIM = 64
ROT_DIM = HEAD_DIM // 4
ROPE_THETA = 500000.0
WINDOW = 128
BLOCK = 128
CONV_DIM = D_MODEL
CONV_WIDTH = 31
D_FF = 4 * D_MODEL
N_BRANCH = 2
EPS = 1e-6
Q_W = N_Q_HEADS * HEAD_DIM
KV_W = N_KV_HEADS * HEAD_DIM
GATE_W = N_BRANCH * D_MODEL
IN_W = Q_W + 2 * KV_W + 2 * CONV_DIM + GATE_W

kernel_name = "hybrid_swa_sink_conformer_conv_gated_block"

def _rmsnorm(x, g):
    xf = x.astype(jnp.float32)
    y = xf * lax.rsqrt(jnp.mean(xf * xf, axis=-1, keepdims=True) + EPS)
    return (y * g.astype(jnp.float32)).astype(x.dtype)

def _layernorm(x, g, b):
    xf = x.astype(jnp.float32)
    mu = jnp.mean(xf, axis=-1, keepdims=True)
    var = jnp.mean(jnp.square(xf - mu), axis=-1, keepdims=True)
    y = (xf - mu) * lax.rsqrt(var + EPS)
    return (y * g.astype(jnp.float32) + b.astype(jnp.float32)).astype(x.dtype)

def _partial_rope(t, positions):
    half = ROT_DIM // 2
    inv_freq = 1.0 / (jnp.float32(ROPE_THETA) ** (jnp.arange(0, ROT_DIM, 2, dtype=jnp.float32) / ROT_DIM))
    ang = positions.astype(jnp.float32)[:, None] * inv_freq[None, :]
    cos = jnp.cos(ang)[None, :, None, :]
    sin = jnp.sin(ang)[None, :, None, :]
    tr = t[..., :ROT_DIM].astype(jnp.float32)
    t1, t2 = tr[..., :half], tr[..., half:]
    rot = jnp.concatenate([t1 * cos - t2 * sin, t2 * cos + t1 * sin], axis=-1)
    return jnp.concatenate([rot.astype(t.dtype), t[..., ROT_DIM:]], axis=-1)

def _band(t):
    b, s, h, d = t.shape
    tb = t.reshape(b, s // BLOCK, BLOCK, h, d)
    prev = jnp.pad(tb[:, :-1], ((0, 0), (1, 0), (0, 0), (0, 0), (0, 0)))
    return jnp.concatenate([prev, tb], axis=2)

def _sliding_window_sink_attention(q, k, v, sinks):
    b, s, _, d = q.shape
    nb = s // BLOCK
    grp = N_Q_HEADS // N_KV_HEADS
    qb = q.reshape(b, nb, BLOCK, N_KV_HEADS, grp, d)
    kb = _band(k)
    vb = _band(v)
    scores = jnp.einsum("bnqkgd,bnskd->bnkgqs", qb, kb).astype(jnp.float32) * (HEAD_DIM ** -0.5)
    i = jnp.arange(BLOCK)[:, None]
    j = jnp.arange(2 * BLOCK)[None, :]
    rel = i + BLOCK - j
    kpos = jnp.arange(nb)[:, None, None] * BLOCK - BLOCK + j[None]
    valid = (rel >= 0) & (rel < WINDOW) & (kpos >= 0)
    scores = jnp.where(valid[None, :, None, None], scores, -jnp.inf)
    sink = jnp.broadcast_to(
        sinks.astype(jnp.float32).reshape(N_KV_HEADS, grp)[None, None, :, :, None, None],
        scores.shape[:-1] + (1,))
    probs = jax.nn.softmax(jnp.concatenate([scores, sink], axis=-1), axis=-1)[..., :-1]
    out = jnp.einsum("bnkgqs,bnskd->bnqkgd", probs.astype(v.dtype), vb)
    return out.reshape(b, s, N_Q_HEADS * d)

def _conformer_conv(u, conv_w, conv_b, norm_g, norm_b, w_conv_out):
    a, gt = jnp.split(u, 2, axis=-1)
    glu = a * jax.nn.sigmoid(gt)
    y = lax.conv_general_dilated(
        glu, conv_w[:, None, :].astype(glu.dtype), window_strides=(1,),
        padding=[(CONV_WIDTH - 1, 0)], dimension_numbers=("NWC", "WIO", "NWC"),
        feature_group_count=CONV_DIM) + conv_b
    y = jax.nn.silu(_layernorm(y, norm_g, norm_b))
    return y @ w_conv_out

def setup_inputs(seed: int = 0) -> dict:
    key = jax.random.key(seed)
    ks = jax.random.split(key, 20)
    f32 = jnp.float32
    n = lambda k, shape, scale: jax.random.normal(k, shape, f32) * scale
    L = DEPTH
    return {
        "x": n(ks[0], (BATCH, SEQ, D_MODEL), 1.0),
        "norm1_g": 1.0 + n(ks[1], (L, D_MODEL), 0.02),
        "w_in": n(ks[2], (L, D_MODEL, IN_W), D_MODEL ** -0.5),
        "gate_b": n(ks[3], (L, GATE_W), 0.02),
        "q_norm_g": 1.0 + n(ks[4], (L, HEAD_DIM), 0.02),
        "k_norm_g": 1.0 + n(ks[5], (L, HEAD_DIM), 0.02),
        "sinks": n(ks[6], (L, N_Q_HEADS), 0.5),
        "w_attn_out": n(ks[7], (L, Q_W, D_MODEL), Q_W ** -0.5),
        "conv_w": n(ks[8], (L, CONV_WIDTH, CONV_DIM), CONV_WIDTH ** -0.5),
        "conv_b": n(ks[9], (L, CONV_DIM), 0.02),
        "conv_norm_g": 1.0 + n(ks[10], (L, CONV_DIM), 0.02),
        "conv_norm_b": n(ks[11], (L, CONV_DIM), 0.02),
        "w_conv_out": n(ks[12], (L, CONV_DIM, D_MODEL), CONV_DIM ** -0.5),
        "w_out": n(ks[13], (L, D_MODEL, D_MODEL), D_MODEL ** -0.5),
        "norm2_g": 1.0 + n(ks[14], (L, D_MODEL), 0.02),
        "w_up": n(ks[15], (L, D_MODEL, D_FF), D_MODEL ** -0.5),
        "w_down": n(ks[16], (L, D_FF, D_MODEL), D_FF ** -0.5),
    }

def reference(x, norm1_g, w_in, gate_b, q_norm_g, k_norm_g, sinks, w_attn_out,
              conv_w, conv_b, conv_norm_g, conv_norm_b, w_conv_out, w_out,
              norm2_g, w_up, w_down):
    b, s, _ = x.shape
    positions = jnp.arange(s, dtype=jnp.int32)
    splits = np.cumsum([Q_W, KV_W, KV_W, 2 * CONV_DIM]).tolist()
    for l in range(DEPTH):
        h = _rmsnorm(x, norm1_g[l])
        proj = h @ w_in[l]
        q, k, v, conv_in, gate_logits = jnp.split(proj, splits, axis=-1)
        q = q.reshape(b, s, N_Q_HEADS, HEAD_DIM)
        k = k.reshape(b, s, N_KV_HEADS, HEAD_DIM)
        v = v.reshape(b, s, N_KV_HEADS, HEAD_DIM)
        q = _partial_rope(_rmsnorm(q, q_norm_g[l]), positions)
        k = _partial_rope(_rmsnorm(k, k_norm_g[l]), positions)
        y_attn = _sliding_window_sink_attention(q, k, v, sinks[l]) @ w_attn_out[l]
        y_conv = _conformer_conv(conv_in, conv_w[l], conv_b[l], conv_norm_g[l],
                                 conv_norm_b[l], w_conv_out[l])
        gates = jax.nn.sigmoid(gate_logits + gate_b[l]).reshape(b, s, N_BRANCH, D_MODEL)
        merged = gates[:, :, 0] * y_attn + gates[:, :, 1] * y_conv
        x = x + merged @ w_out[l]
        hn = _rmsnorm(x, norm2_g[l])
        x = x + jnp.square(jax.nn.relu(hn @ w_up[l])) @ w_down[l]
    return x


_drawn_inputs = setup_inputs


def setup_inputs(seed=0):
    import zlib

    import numpy as np

    out = dict(_drawn_inputs(seed))
    spreads = {}
    factors = {'norm1_g': 6.23,
     'gate_b': 8.0,
     'q_norm_g': 8.0,
     'k_norm_g': 8.0,
     'sinks': 200.0,
     'conv_b': 15.528,
     'conv_norm_g': 79.833,
     'conv_norm_b': 76.433,
     'norm2_g': 8.784}
    for name, (base, spread) in spreads.items():
        noise = np.random.default_rng([zlib.crc32(name.encode()), seed]).standard_normal(out[name].shape)
        drawn = base * np.exp(spread * noise) if base else spread * noise
        out[name] = __import__('jax').numpy.asarray(drawn.astype(out[name].dtype))
    for name, factor in factors.items():
        out[name] = (out[name] * factor).astype(out[name].dtype)
    return out
```

```python
from contextlib import ExitStack

import numpy as np

import concourse.bass as bass
from concourse import mybir

F32 = mybir.dt.float32
F32R = mybir.dt.float32r
ALU = mybir.AluOpType
ACT = mybir.ActivationFunctionType
AX = mybir.AxisListType

P = 128
D = 1024
S = 1024
KC = D // P
TT = S // P
HN = 512
N_Q, N_KV, HD = 16, 4, 64
GRP = N_Q // N_KV
ROT = HD // 4
HALF = ROT // 2
THETA = 500000.0
Q_W = N_Q * HD
KV_W = N_KV * HD
TAPS = 31
PAD = TAPS - 1
FF = 4 * D
EPS = 1e-6
COL_A = Q_W + 2 * KV_W
COL_G = COL_A + D
COL_GATE = COL_A + 2 * D
COL_GATE2 = COL_GATE + D
SLOTS = 4
FFG = 256
NFG = FF // FFG
NEG = -1e30

N_QKV, N_GA, N_YA, N_CONV, N_YB, N_OUT, N_MLP = 12, 8, 8, 24, 8, 8, 4 * NFG
T_QKV = 0
T_GA = T_QKV + N_QKV
T_YA = T_GA + N_GA
T_CONV = T_YA + N_YA
T_YB = T_CONV + N_CONV
T_OUT = T_YB + N_YB
T_MLP = T_OUT + N_OUT
N_TILES = T_MLP + N_MLP

V_N1, V_GA, V_GB, V_CB, V_CG, V_CNB, V_N2 = 0, 8, 16, 24, 32, 40, 48
N_VEC = 56


class Count:

    def __init__(self, engine, sem):
        self.engine, self.sem, self.n = engine, sem, 0

    def add(self, instruction):
        instruction.then_inc(self.sem, 1)
        self.n = self.n + 1
        return self.n

    def wait(self, n=None):
        self.engine.wait_ge(self.sem, self.n if n is None else n)


def rope_tables():
    power = np.power(np.float32(THETA), np.arange(0, ROT, 2, dtype=np.float32) / np.float32(ROT))
    angle = np.arange(S, dtype=np.float32)[:, None] * (np.float32(1.0) / power.astype(np.float32))[None, :]
    return np.cos(angle).astype(np.float32), np.sin(angle).astype(np.float32)


def hybrid_block(nc, x, norm1_g, w_in, gate_b, q_norm_g, k_norm_g, sinks, w_attn_out, conv_w, conv_b,
                 conv_norm_g, conv_norm_b, w_conv_out, w_out, norm2_g, w_up, w_down, cos_t, sin_t, out):
    x_tiles = x[0].rearrange("(t p) d -> t p d", p=P)
    out_tiles = out[0].rearrange("(t p) d -> t p d", p=P)
    base = 16896
    KB = 1024

    with ExitStack() as ctx:
        def sb(name, kb, shape, dt=F32):
            return nc.alloc_sbuf_tensor_at(name, shape, dt, offset=base + int(kb * KB))

        def sem(name):
            return ctx.enter_context(nc.semaphore(name))

        h_hi = sb("h_hi", 0, [P, KC, S], F32R)
        h_lo = sb("h_lo", 32, [P, KC, S], F32R)
        c_hi = sb("c_hi", 0, [P, KC, S], F32R)
        c_lo = sb("c_lo", 32, [P, KC, S], F32R)
        hn_hi = sb("hn_hi", 0, [P, KC, S], F32R)
        hn_lo = sb("hn_lo", 32, [P, KC, S], F32R)
        x_tok = sb("x_tok", 64, [P, TT, D])
        q_tok = sb("q_tok", 64, [P, TT, Q_W])
        o_raw = sb("o_raw", 64, [P, TT, KC, P])
        o_lo = sb("o_lo", 64, [P, TT, KC, P], F32R)
        y = sb("y", 64, [P, KC, S])
        x2 = sb("x2", 64, [P, TT, D])
        kv_tok = sb("kv_tok", 96, [P, TT, 2 * KV_W])
        cos_sb = sb("cos_sb", 112, [P, TT, HALF])
        sin_sb = sb("sin_sb", 112.25, [P, TT, HALF])
        gq = sb("gq", 112.5, [P, HD])
        gk = sb("gk", 112.75, [P, HD])
        ga = sb("ga", 96, [P, KC, S])
        m_hi = sb("m_hi", 96, [P, KC, S], F32R)
        xn2 = sb("xn2", 96, [P, TT, D])
        a_hi = [sb(f"a_hi{i}", 96 + 16 * i, [P, 2, S], F32R) for i in range(2)]
        a_lo = [sb(f"a_lo{i}", 104 + 16 * i, [P, 2, S], F32R) for i in range(2)]
        w_hi = [sb(f"w_hi{i}", 128 + 8 * i, [P, D], F32R) for i in range(SLOTS)]
        w_raw = [sb(f"w_raw{i}", 132 + 8 * i, [P, D]) for i in range(SLOTS)]
        w_lo = [sb(f"w_lo{i}", 132 + 8 * i, [P, D], F32R) for i in range(SLOTS)]
        junk = sb("junk", 160, [P, D])
        cw_rows = sb("cw_rows", 164, [32, D])
        vec_rows = sb("vec_rows", 168, [N_VEC, P])
        k_t = sb("k_t", 160, [P, 2, S])
        v_hi = sb("v_hi", 168, [P, TT, KV_W], F32R)
        v_lo = sb("v_lo", 176, [P, TT, KV_W], F32R)
        squares = sb("squares", 184, [P, 4, HN])
        rope_tmp = [sb(f"rope_tmp{i}", 192 + 2 * i, [P, TT, 8, HALF]) for i in range(4)]
        head_ss = sb("head_ss", 200, [P, TT, 8])
        head_rs = sb("head_rs", 200.25, [P, TT, 8])
        probs = [sb(f"probs{i}", 184 + 4 * i, [P, GRP, 2 * P]) for i in range(2)]
        pt_hi = sb("pt_hi", 192, [P, 2, HN], F32R)
        pt_lo = sb("pt_lo", 196, [P, 2, HN], F32R)
        q_t = [sb(f"q_t{i}", 200 + 2 * i, [P, HN]) for i in range(2)]
        mask = sb("mask", 204, [P, 2 * P])
        o_hi = sb("o_hi", 160, [P, TT, KC, P], F32R)
        gb = sb("gb", 160, [P, KC, S])
        m_lo = sb("m_lo", 160, [P, KC, S], F32R)
        GLU_W = PAD + S + 2
        glu = [sb(f"glu{i}", 192 + 4.125 * i, [P, GLU_W]) for i in range(2)]
        sq_y = [sb(f"sq_y{i}", 192 + 4 * i, [P, S]) for i in range(2)]
        sig = [sb(f"sig{i}", 192 + 4 * i, [P, S]) for i in range(2)]
        ln_rs = sb("ln_rs", 200, [P, S])
        junk2 = sb("junk2", 192, [P, D])
        relu_t = [sb(f"relu_t{i}", 160 + 4 * i, [P, S]) for i in range(2)]
        relu_sq = [sb(f"relu_sq{i}", 168 + 4 * i, [P, S]) for i in range(2)]
        small = 205 * KB
        ident = sb("ident", small / KB, [P, P])
        mean_w = sb("mean_w", (small + 512) / KB, [P, P])
        vec = sb("vec", (small + 1024) / KB, [P, N_VEC])
        cw = sb("cw", (small + 1248) / KB, [P, KC, 32])
        sink = sb("sink", (small + 2272) / KB, [P, N_Q])
        stat = sb("stat", (small + 2336) / KB, [P, 48])

        ps = ctx.enter_context(nc.psum_tensor("ps", [P, 8, HN], F32))

        def bank(b, n=1):
            return ps[:, b:b + n, :].rearrange("p b n -> p (b n)")

        s_x = [sem(f"x_landed{t}") for t in range(TT)]
        s_const = sem("constants_landed")
        s_cwzero = sem("conv_taps_zeroed")
        s_ident = sem("identity_built")
        s_landed = [sem(f"weights_landed{i}") for i in range(SLOTS)]
        s_seen = sem("weights_seen")
        s_hi = sem("weights_hi_split")
        s_split = sem("weights_split")
        s_begun = sem("tiles_begun")
        s_dve = sem("vector_steps")
        s_tab = sem("tables_transposed")
        s_tabr = sem("tables_ready")
        s_xss = sem("x_squares_summed")
        s_xms = sem("x_mean_square")
        s_xrt = sem("x_root")
        s_xn = sem("x_normalised")
        s_xT = sem("x_transposed")
        s_hhi = sem("h_hi_ready")
        s_h = sem("h_ready")
        s_qkvp = sem("qkv_partial")
        s_qkvs = sem("qkv_summed")
        s_sq = sem("head_squares")
        s_ss = sem("head_squares_summed")
        s_ms = sem("head_mean_square")
        s_rt = sem("head_root")
        s_qk = sem("heads_ready")
        s_vhi = sem("v_hi_ready")
        s_v = sem("v_ready")
        s_kT = sem("k_transposed")
        s_kTr = sem("k_t_ready")
        s_qT = sem("q_transposed")
        s_qTr = sem("q_t_ready")
        s_sc = sem("scores")
        s_mx = sem("scores_masked")
        s_exp = sem("exps")
        s_pn = sem("probs_normalised")
        s_pT = sem("probs_transposed")
        s_pThi = sem("pt_hi_ready")
        s_pTr = sem("pt_ready")
        s_pv = sem("values_mixed")
        s_oe = sem("o_stored")
        s_ga = sem("gate_a_logits")
        s_gae = sem("gate_a_stored")
        s_gas = sem("gate_a_sigmoid")
        s_ohi = sem("o_hi_ready")
        s_o = sem("o_ready")
        s_ya = sem("y_attn")
        s_ma = sem("attn_merged")
        s_ca = sem("conv_a")
        s_cg = sem("conv_gate")
        s_cs = sem("conv_sigmoid")
        s_glu = sem("glu_ready")
        s_gfree = sem("glu_buffers_free")
        s_gbl = sem("gate_b_logits")
        s_gb = sem("gate_b_ready")
        s_mean = sem("mean_ready")
        s_yc = sem("centred")
        s_ysq = sem("centred_squares")
        s_ysu = sem("squares_used")
        s_var = sem("variance_ready")
        s_std = sem("std_ready")
        s_z = sem("ln_scaled")
        s_sw = sem("ln_activated")
        s_c = sem("conv_out_ready")
        s_chi = sem("c_hi_ready")
        s_clo = sem("c_ready")
        s_yb = sem("y_conv")
        s_mb = sem("y_conv_read")
        s_ms2 = sem("merged")
        s_mhi = sem("m_hi_ready")
        s_m = sem("m_ready")
        s_x2in = sem("x_reloaded")
        s_op = sem("out_partial")
        s_os = sem("out_summed")
        s_x2ss = sem("x2_squares_summed")
        s_x2ms = sem("x2_mean_square")
        s_x2rt = sem("x2_root")
        s_x2n = sem("x2_normalised")
        s_x2T = sem("x2_transposed")
        s_hnhi = sem("hn_hi_ready")
        s_hn = sem("hn_ready")
        s_up = sem("up_done")
        s_relu = sem("relu_done")
        s_rsq = sem("relu_squared")
        s_ahi = sem("a_hi_ready")
        s_a = sem("a_ready")
        s_dn = sem("down_partial")
        s_ds = sem("down_summed")
        s_out = sem("output_stored")

        block = ctx.enter_context(nc.Block())

        def column_tile(w, c0):
            return w.rearrange("(k p) n -> p k n", p=P)[:, :, bass.ds(c0, P)]

        def row_tile(w, k0, c0):
            return w[bass.ds(k0, 2 * P), bass.ds(c0, HN)].rearrange("(k p) n -> p k n", p=P)

        @block.sync
        def _(sp):
            for t in range(TT):
                sp.dma_start(x_tok[:, t, :], x_tiles[t]).then_inc(s_x[t], 16)

            def load(n, slot, src, wait=True):
                if wait:
                    sp.wait_ge(s_begun, n - SLOTS + 2)
                k = src.shape[1]
                sp.dma_start(w_raw[slot][:, :].rearrange("p (k n) -> p k n", k=k), src).then_inc(s_landed[slot], 16)

            for g, c0 in enumerate((Q_W, 0, HN)):
                for kp in range(4):
                    load(4 * g + kp, kp, row_tile(w_in[0], 2 * P * kp, c0), wait=g > 0)
            with sp.Fori(0, N_GA // SLOTS) as i:
                for s in range(SLOTS):
                    load(T_GA + SLOTS * i + s, s, column_tile(w_in[0], COL_GATE + (SLOTS * i + s) * P))
            with sp.Fori(0, N_YA // SLOTS) as i:
                for s in range(SLOTS):
                    load(T_YA + SLOTS * i + s, s, column_tile(w_attn_out[0], (SLOTS * i + s) * P))
            with sp.Fori(0, 2) as i:
                for s in range(12):
                    c = 4 * i + s // 3
                    load(T_CONV + 12 * i + s, s % SLOTS,
                         column_tile(w_in[0], (COL_A, COL_G, COL_GATE2)[s % 3] + c * P))
            with sp.Fori(0, N_YB // SLOTS) as i:
                for s in range(SLOTS):
                    load(T_YB + SLOTS * i + s, s, column_tile(w_conv_out[0], (SLOTS * i + s) * P))
            sp.wait_ge(s_clo, KC)
            for t in range(TT):
                sp.dma_start(x2[:, t, :], x_tiles[t]).then_inc(s_x2in, 16)
            with sp.Fori(0, 2) as i:
                for s in range(SLOTS):
                    load(T_OUT + SLOTS * i + s, s, row_tile(w_out[0], 2 * P * s, i * HN))

            for s in range(2):
                load(T_MLP + s, s, column_tile(w_up[0], s * P))
            with sp.Fori(0, NFG - 1) as g:
                for s in range(2):
                    load(T_MLP + 2 + 4 * g + s, 2 + s, column_tile(w_up[0], (2 * g + 2 + s) * P))
                for s in range(2):
                    load(T_MLP + 4 + 4 * g + s, s, row_tile(w_down[0], g * FFG, s * HN))
            for s in range(2):
                load(N_TILES - 2 + s, 2 + s, row_tile(w_down[0], FF - FFG, s * HN))
            for t in range(TT):
                sp.wait_ge(s_ds, 16 * (NFG - 1) + 8 + t + 1)
                sp.dma_start(out_tiles[t], x2[:, t, :]).then_inc(s_out, 16)
            sp.wait_ge(s_out, 16 * TT)

        @block.gpsimd
        def _(pool):
            pool.memset(cw_rows[:, :], 0.0).then_inc(s_cwzero, 1)
            pool.memset(ident[:, :], 0.0).then_inc(s_ident, 1)
            pool.memset(mean_w[:, :], 1.0 / D).then_inc(s_ident, 1)
            pool.memset(mask[:, :], 0.0).then_inc(s_ident, 1)
            pool.wait_ge(s_ident, 3)
            pool.affine_select(out=ident[:, :], in_=ident[:, :], compare_op=ALU.not_equal, fill=1.0,
                               base=0, pattern=[[-1, P]], channel_multiplier=1).then_inc(s_ident, 1)
            pool.affine_select(out=mask[:, 0:P], in_=mask[:, 0:P], compare_op=ALU.is_gt, fill=NEG,
                               base=0, pattern=[[1, P]], channel_multiplier=-1).then_inc(s_ident, 1)
            pool.affine_select(out=mask[:, P:2 * P], in_=mask[:, P:2 * P], compare_op=ALU.is_ge, fill=NEG,
                               base=0, pattern=[[-1, P]], channel_multiplier=1).then_inc(s_ident, 1)
            with pool.Fori(0, N_TILES // SLOTS) as i:
                for s in range(SLOTS):
                    pool.wait_ge(s_landed[s], 16 * i + 16)
                    pool.sem_inc(s_seen, 1)
                    pool.tensor_copy(w_hi[s][:, :], w_raw[s][:, :]).then_inc(s_hi, 1)
                    pool.wait_ge(s_hi, SLOTS * i + s + 1)
                    pool.tensor_tensor(w_lo[s][:, :], w_raw[s][:, :], w_hi[s][:, :].bitcast(F32),
                                       ALU.subtract).then_inc(s_split, 1)

        @block.tensor
        def _(pe):
            def column_product(n, slot, b, rhs_hi, rhs_lo, ks=range(KC)):
                pe.wait_ge(s_split, n + 1)
                wh = w_hi[slot][:, :].rearrange("p (k m) -> p k m", k=KC)
                wl = w_lo[slot][:, :].rearrange("p (k m) -> p k m", k=KC)
                for k in ks:
                    first, last = k == 0, k == KC - 1
                    for h in range(2):
                        o = ps[:, b + h, :]
                        mm = pe.matmul(o, wh[:, k, :], rhs_hi(k, h), start=first, stop=False)
                        if first and h == 0:
                            mm.then_inc(s_begun, 1)
                        pe.matmul(o, wh[:, k, :], rhs_lo(k, h), start=False, stop=False)
                    for h in range(2):
                        o = ps[:, b + h, :]
                        mm = pe.matmul(o, wl[:, k, :], rhs_hi(k, h), start=False, stop=last)
                return mm

            def row_product(b, lhs_hi, lhs_lo, slot, begins):
                wh = w_hi[slot][:, :].rearrange("p (k n) -> p k n", k=2)
                wl = w_lo[slot][:, :].rearrange("p (k n) -> p k n", k=2)
                for k in range(2):
                    mm = pe.matmul(ps[:, b, :], lhs_hi(k), wh[:, k, :], start=k == 0, stop=False)
                    if begins and k == 0:
                        mm.then_inc(s_begun, 1)
                    pe.matmul(ps[:, b, :], lhs_hi(k), wl[:, k, :], start=False, stop=False)
                    mm = pe.matmul(ps[:, b, :], lhs_lo(k), wh[:, k, :], start=False, stop=k == 1)
                return mm

            def halves(a):
                return lambda k, h: a[:, k, h * HN:(h + 1) * HN]

            pe.wait_ge(s_ident, 4)
            pe.wait_ge(s_const, 16 * 12)
            pe.transpose(ps[:, 7, 0:N_VEC], vec_rows[:, :], ident[0:N_VEC, 0:N_VEC])
            for c in range(KC):
                mm = pe.transpose(ps[:, 6, 32 * c:32 * c + 32], cw_rows[:, c * P:(c + 1) * P], ident[0:32, 0:32])
            mm.then_inc(s_tab, 1)

            def transposed(src, half, c, i, free, done, ready):
                if i >= 4:
                    pe.wait_ge(free, i - 3)
                if c == 0:
                    pe.wait_ge(ready, 4 * half + 4)
                for j in range(4):
                    mm = pe.transpose(ps[:, i % 4, j * P:(j + 1) * P], src[:, 4 * half + j, c * P:(c + 1) * P],
                                      ident[:, :])
                mm.then_inc(done, 1)

            for half in range(2):
                for c in range(KC):
                    transposed(x_tok, half, c, half * KC + c, s_h, s_xT, s_xn)

            pe.wait_ge(s_h, 2 * KC)
            j = 0
            for g in range(3):
                for kp in range(4):
                    n = 4 * g + kp
                    pe.wait_ge(s_split, n + 1)
                    for t in range(TT):
                        if j >= 4:
                            pe.wait_ge(s_qkvs, j - 3)
                        mm = row_product(j % 4, lambda k: h_hi[:, 2 * kp + k, t * P:(t + 1) * P],
                                         lambda k: h_lo[:, 2 * kp + k, t * P:(t + 1) * P], kp, t == 0)
                        mm.then_inc(s_qkvp, 1)
                        j += 1
                if g == 1:
                    pe.wait_ge(s_qk, 1)
                    for p in range(2):
                        for half in range(2):
                            for t in range(4):
                                mm = pe.transpose(ps[:, 4 + 2 * p + half, t * P:(t + 1) * P],
                                                  kv_tok[:, 4 * half + t, p * P:(p + 1) * P], ident[:, :])
                            mm.then_inc(s_kT, 1)

            def q_unit(u):
                b, p = u // 2, u % 2
                if u >= 1:
                    pe.wait_ge(s_qTr, u)
                for j in range(GRP):
                    c0 = (p * GRP + j) * P
                    mm = pe.transpose(ps[:, 3, j * P:(j + 1) * P], q_tok[:, b, c0:c0 + P], ident[:, :])
                mm.then_inc(s_qT, 1)

            def scores(G):
                b, kv = G // N_KV, G % N_KV
                p, s = kv // 2, kv % 2
                r = slice(64 * s, 64 * s + 64)
                pe.wait_ge(s_qTr, G // 2 + 1)
                if G:
                    pe.wait_ge(s_mx, G)
                keys = slice(max(b - 1, 0) * P, (b + 1) * P)
                lo = P if b == 0 else 0
                for j in range(GRP):
                    c0 = (j % 2) * 256
                    mm = pe.matmul(ps[:, 4 + j // 2, c0 + lo:c0 + 256], q_t[(G // 2) % 2][r, j * P:(j + 1) * P],
                                   k_t[r, p, keys], start=True, stop=True)
                mm.then_inc(s_sc, 1)

            def turn_probs(G):
                pe.wait_ge(s_pn, G + 1)
                if G:
                    pe.wait_ge(s_pTr, G)
                for hf in range(1 if G < N_KV else 0, 2):
                    for j in range(GRP):
                        mm = pe.transpose(ps[:, 6 + hf, j * P:(j + 1) * P],
                                          probs[G % 2][:, j, hf * P:(hf + 1) * P], ident[:, :])
                mm.then_inc(s_pT, 1)

            def mix_values(G):
                b, kv = G // N_KV, G % N_KV
                pe.wait_ge(s_pTr, G + 1)
                if G:
                    pe.wait_ge(s_oe, G)
                else:
                    pe.wait_ge(s_v, 1)
                hs = [1] if b == 0 else [0, 1]
                for hf in hs:
                    vh, vl = (v[:, b - 1 + hf, kv // 2 * P:(kv // 2 + 1) * P] for v in (v_hi, v_lo))
                    pe.matmul(ps[:, 2, :], vh, pt_hi[:, hf, :], start=hf == hs[0], stop=False)
                    pe.matmul(ps[:, 2, :], vh, pt_lo[:, hf, :], start=False, stop=False)
                    mm = pe.matmul(ps[:, 2, :], vl, pt_hi[:, hf, :], start=False, stop=hf == 1)
                mm.then_inc(s_pv, 1)

            pe.wait_ge(s_qkvs, 96)
            pe.wait_ge(s_kTr, 4)
            NG = TT * N_KV
            def gate_part(f, part):
                if part == 0 and f:
                    pe.wait_ge(s_gae, f)
                mm = column_product(T_GA + f, f % SLOTS, 0, halves(h_hi), halves(h_lo), range(2 * part, 2 * part + 2))
                if part == 3:
                    mm.then_inc(s_ga, 1)

            for part in range(4):
                gate_part(0, part)
            pe.wait_ge(s_qk, 3)
            q_unit(0)
            q_unit(1)
            for G in range(NG + 2):
                if G < NG:
                    scores(G)
                    if G % 4 == 2 and G + 2 < NG:
                        q_unit((G + 2) // 2)
                    if G % 4 == 3 and G + 1 < NG:
                        q_unit((G + 1) // 2 + 1)
                if G < NG - 4:
                    gate_part(1 + G // 4, G % 4)
                if 2 <= G:
                    mix_values(G - 2)
                if 1 <= G <= NG:
                    turn_probs(G - 1)

            o_rhs = lambda o: (lambda k, h: o[:, 4 * h:4 * h + 4, k, :])
            pe.wait_ge(s_o, TT)
            pe.wait_ge(s_gae, KC)

            def eight_tiles(first_tile, rhs_hi, rhs_lo, done, free):
                with pe.Fori(0, 2) as i:
                    for s in range(SLOTS):
                        f = SLOTS * i + s
                        if s >= 2:
                            pe.wait_ge(free, f - 1)
                        mm = column_product(first_tile + f, s, 2 * (s % 2), rhs_hi, rhs_lo)
                        mm.then_inc(done, 1)
                    pe.wait_ge(free, SLOTS * i + SLOTS)

            eight_tiles(T_YA, o_rhs(o_hi), o_rhs(o_lo), s_ya, s_ma)

            with pe.Fori(0, 2) as i:
                for u in range(4):
                    c = 4 * i + u
                    n = T_CONV + 3 * c
                    mm = column_product(n, (3 * u) % SLOTS, 0, halves(h_hi), halves(h_lo))
                    mm.then_inc(s_ca, 1)
                    mm = column_product(n + 1, (3 * u + 1) % SLOTS, 2, halves(h_hi), halves(h_lo))
                    mm.then_inc(s_cg, 1)
                    if u:
                        pe.wait_ge(s_gb, c)
                    mm = column_product(n + 2, (3 * u + 2) % SLOTS, 4, halves(h_hi), halves(h_lo))
                    mm.then_inc(s_gbl, 1)
                    pe.wait_ge(s_glu, c + 1)
                pe.wait_ge(s_gb, 4 * i + 4)

            for c in range(KC):
                pe.wait_ge(s_gfree, c + 3)
                for h in range(2):
                    mm = pe.matmul(ps[:, h, :], mean_w[:, :], y[:, c, h * HN:(h + 1) * HN], start=c == 0, stop=c == KC - 1)
            mm.then_inc(s_mean, 1)
            for c in range(KC):
                pe.wait_ge(s_ysq, c + 1)
                for h in range(2):
                    mm = pe.matmul(ps[:, 2 + h, :], mean_w[:, :], sq_y[c % 2][:, h * HN:(h + 1) * HN],
                                   start=c == 0, stop=c == KC - 1)
                mm.then_inc(s_ysu, 1)

            pe.wait_ge(s_clo, KC)
            eight_tiles(T_YB, halves(c_hi), halves(c_lo), s_yb, s_mb)

            pe.wait_ge(s_m, KC)
            with pe.Fori(0, 2) as i:
                for kp in range(SLOTS):
                    pe.wait_ge(s_split, T_OUT + SLOTS * i + kp + 1)
                    for t in range(TT):
                        j = kp * TT + t
                        if j >= 4:
                            pe.wait_ge(s_os, 32 * i + j - 3)
                        mm = row_product(t % 4, lambda k: m_hi[:, 2 * kp + k, t * P:(t + 1) * P],
                                         lambda k: m_lo[:, 2 * kp + k, t * P:(t + 1) * P], kp, t == 0)
                        mm.then_inc(s_op, 1)
                pe.wait_ge(s_os, 32 * i + 32)

            for half in range(2):
                for c in range(KC):
                    transposed(xn2, half, c, half * KC + c, s_hn, s_x2T, s_x2n)
            pe.wait_ge(s_hn, 2 * KC)

            def up(g, n, slot0):
                for s in range(2):
                    if not (isinstance(g, int) and g == 0):
                        pe.wait_ge(s_relu, 2 * g + s - 1)
                    mm = column_product(n + s, slot0 + s, 2 * s, halves(hn_hi), halves(hn_lo))
                    mm.then_inc(s_up, 1)

            def down(g, parity, n, slot0):
                pe.wait_ge(s_a, 2 * g + 2)
                for s in range(2):
                    pe.wait_ge(s_split, n + s + 1)
                    for t in range(TT):
                        if not (isinstance(g, int) and g == 0 and s == 0 and t < 4):
                            pe.wait_ge(s_ds, 16 * g + 8 * s + t - 3)
                        mm = row_product(4 + t % 4, lambda k: a_hi[parity][:, k, t * P:(t + 1) * P],
                                         lambda k: a_lo[parity][:, k, t * P:(t + 1) * P], slot0 + s, t == 0)
                        mm.then_inc(s_dn, 1)

            up(0, T_MLP, 0)
            up(1, T_MLP + 2, 2)
            down(0, 0, T_MLP + 4, 0)
            with pe.Fori(0, (NFG - 2) // 2) as i:
                for par in range(2):
                    g = 2 * i + par + 1
                    up(g + 1, T_MLP + 2 + 4 * g, 2)
                    down(g, (par + 1) % 2, T_MLP + 4 + 4 * g, 0)
            down(NFG - 1, 1, N_TILES - 2, 2)

        @block.scalar
        def _(act):
            for r, v in ((V_N1, norm1_g[0]), (V_GA, gate_b[0]), (V_CB, conv_b[0]),
                         (V_CG, conv_norm_g[0]), (V_CNB, conv_norm_b[0]), (V_N2, norm2_g[0])):
                n = v.shape[0] // P
                act.dma_start(vec_rows[r:r + n, :], v.rearrange("(r c) -> r c", c=P)).then_inc(s_const, 16)
            act.wait_ge(s_cwzero, 1)
            act.dma_start(cw_rows[0:TAPS, :], conv_w[0]).then_inc(s_const, 16)
            act.dma_start(gq[:, :], q_norm_g.partition_broadcast(P)).then_inc(s_const, 16)
            act.dma_start(gk[:, :], k_norm_g.partition_broadcast(P)).then_inc(s_const, 16)
            act.dma_start(sink[:, :], sinks.partition_broadcast(P)).then_inc(s_const, 16)
            act.dma_start(cos_sb[:, :, :], cos_t.rearrange("(t p) h -> p t h", p=P)).then_inc(s_const, 16)
            act.dma_start(sin_sb[:, :, :], sin_t.rearrange("(t p) h -> p t h", p=P)).then_inc(s_const, 16)

            def row_squares(src, t, ss, done, trash=junk):
                act.activation(trash[:, :], src[:, t, :], ACT.Square, accum_out=ss).then_inc(done, 1)

            for half in range(2):
                for t in range(4 * half, 4 * half + 4):
                    act.wait_ge(s_x[t], 16)
                    if t:
                        act.wait_ge(s_xss, t)
                    row_squares(x_tok, t, stat[:, t:t + 1], s_xss)
                act.wait_ge(s_xms, half + 1)
                act.activation(stat[:, 8 + 4 * half:12 + 4 * half], stat[:, 4 * half:4 * half + 4],
                               ACT.Sqrt).then_inc(s_xrt, 1)

            act.wait_ge(s_tabr, 2)
            for i in range(2 * KC):
                half, c = i // KC, i % KC
                act.wait_ge(s_xT, i + 1)
                act.activation(h_hi[:, c, half * HN:(half + 1) * HN], ps[:, i % 4, :], ACT.Copy,
                               scale=vec[:, V_N1 + c:V_N1 + c + 1]).then_inc(s_hhi, 1)

            def head_squares(tok, c0, heads, summed, i0):
                for th in range(2):
                    act.wait_ge(s_qkvs, summed + 4 * th + 4)
                    if i0 + th:
                        act.wait_ge(s_ss, i0 + th)
                    act.activation(squares[:, :, 0:heads * HD], tok[:, 4 * th:4 * th + 4, c0:c0 + heads * HD],
                                   ACT.Square).then_inc(s_sq, 1)

            def head_root(i, heads):
                act.wait_ge(s_ms, i + 1)
                act.activation(head_rs[:, :, 0:heads], head_ss[:, :, 0:heads], ACT.Sqrt).then_inc(s_rt, 1)

            head_squares(kv_tok, 0, N_KV, 24, 0)
            act.wait_ge(s_qkvs, 32)
            act.activation(v_hi[:, :, :], kv_tok[:, :, KV_W:2 * KV_W], ACT.Copy).then_inc(s_vhi, 1)
            head_root(0, N_KV)
            head_squares(q_tok, 0, 8, 32 + 24, 2)
            head_root(1, 8)
            for i in range(4):
                act.wait_ge(s_kT, i + 1)
                act.activation(k_t[:, i // 2, (i % 2) * HN:(i % 2 + 1) * HN], ps[:, 4 + i, :],
                               ACT.Copy).then_inc(s_kTr, 1)
            head_squares(q_tok, HN, 8, 64 + 24, 4)
            head_root(2, 8)

            def gate_store(f):
                act.wait_ge(s_ga, f + 1)
                if f == 0:
                    act.wait_ge(s_v, 1)
                    act.wait_ge(s_kT, 4)
                act.activation(ga[:, f, :], bank(0, 2), ACT.Copy).then_inc(s_gae, 1)

            def q_store(u):
                act.wait_ge(s_qT, u + 1)
                if u == 0:
                    act.wait_ge(s_qk, 3)
                if u >= 2:
                    act.wait_ge(s_sc, 2 * (u - 1))
                act.activation(q_t[u % 2][:, :], ps[:, 3, :], ACT.Copy).then_inc(s_qTr, 1)

            def exps(G):
                b, kv = G // N_KV, G % N_KV
                i = G % 2
                lo = P if b == 0 else 0
                act.wait_ge(s_mx, G + 1)
                for j in range(GRP):
                    pr = probs[i][:, j, lo:]
                    act.activation(pr, pr, ACT.Exp, bias=stat[:, 4 * i + j:4 * i + j + 1],
                                   accum_out=stat[:, 8 + 4 * i + j:9 + 4 * i + j])
                act.activation(stat[:, 16 + 4 * i:20 + 4 * i], stat[:, 16 + 4 * i:20 + 4 * i], ACT.Exp).then_inc(s_exp, 1)

            def store_o(G):
                b, kv = G // N_KV, G % N_KV
                act.wait_ge(s_pv, G + 1)
                r0 = 64 * (kv % 2)
                for r in range(2):
                    src = ps[r0:r0 + 64, 2, :].rearrange("p (jj s n) -> p jj s n", jj=2, s=2)[:, :, r, :]
                    ins = act.activation(o_raw[64 * r:64 * r + 64, b, 2 * kv:2 * kv + 2, :], src, ACT.Copy)
                ins.then_inc(s_oe, 1)

            def pt_store(G):
                lo = 1 if G < N_KV else 0
                act.wait_ge(s_pT, G + 1)
                if G:
                    act.wait_ge(s_pv, G)
                act.activation(pt_hi[:, lo:, :], ps[:, 6 + lo:8, :], ACT.Copy).then_inc(s_pThi, 1)

            NG = TT * N_KV
            gate_store(0)
            q_store(0)
            q_store(1)
            for G in range(NG + 2):
                if G < NG:
                    if G % 4 == 2 and G + 2 < NG:
                        q_store((G + 2) // 2)
                    if G % 4 == 3 and G + 1 < NG:
                        q_store((G + 1) // 2 + 1)
                    exps(G)
                if G < NG - 4 and G % 4 == 3:
                    gate_store(1 + G // 4)
                if G >= 2:
                    store_o(G - 2)
                if 1 <= G <= NG:
                    pt_store(G - 1)

            act.wait_ge(s_oe, NG)
            for t in range(TT):
                act.activation(o_hi[:, t, :, :], o_raw[:, t, :, :], ACT.Copy).then_inc(s_ohi, 1)
            act.wait_ge(s_gae, KC)
            for f in range(KC):
                act.activation(ga[:, f, :], ga[:, f, :], ACT.Sigmoid,
                               bias=vec[:, V_GA + f:V_GA + f + 1]).then_inc(s_gas, 1)

            with act.Fori(0, KC // 2) as i:
                for u in range(2):
                    c = 2 * i + u
                    act.wait_ge(s_cg, c + 1)
                    act.wait_ge(s_gfree, c + 1)
                    act.activation(glu[u][:, PAD:PAD + S], bank(2, 2), ACT.Sigmoid).then_inc(s_cs, 1)
                    act.wait_ge(s_gbl, c + 1)
                    act.activation(gb[:, c, :], bank(4, 2), ACT.Sigmoid,
                                   bias=vec[:, bass.ds(V_GB + c, 1)]).then_inc(s_gb, 1)

            for c in range(KC):
                act.wait_ge(s_yc, c + 1)
                if c >= 2:
                    act.wait_ge(s_ysu, c - 1)
                act.activation(sq_y[c % 2][:, :], y[:, c, :], ACT.Square).then_inc(s_ysq, 1)
            act.wait_ge(s_var, 1)
            act.activation(ln_rs[:, :], ln_rs[:, :], ACT.Sqrt).then_inc(s_std, 1)

            def c_store(c):
                act.wait_ge(s_c, c + 1)
                act.activation(c_hi[:, c, :], y[:, c, :], ACT.Copy).then_inc(s_chi, 1)

            for c in range(KC):
                act.wait_ge(s_z, c + 1)
                if c >= 2:
                    act.wait_ge(s_c, c - 1)
                g, b = vec[:, V_CG + c:V_CG + c + 1], vec[:, V_CNB + c:V_CNB + c + 1]
                act.activation(sig[c % 2][:, :], y[:, c, :], ACT.Sigmoid, bias=b, scale=g)
                act.activation(y[:, c, :], y[:, c, :], ACT.Identity, bias=b, scale=g).then_inc(s_sw, 1)
                if c:
                    c_store(c - 1)
            c_store(KC - 1)

            for f in range(KC):
                act.wait_ge(s_ms2, f + 1)
                act.activation(m_hi[:, f, :], gb[:, f, :], ACT.Copy).then_inc(s_mhi, 1)

            for half in range(2):
                for t in range(4 * half, 4 * half + 4):
                    act.wait_ge(s_os, 32 + 24 + t + 1)
                    if t:
                        act.wait_ge(s_x2ss, t)
                    row_squares(x2, t, stat[:, t:t + 1], s_x2ss, junk2)
                act.wait_ge(s_x2ms, half + 1)
                act.activation(stat[:, 8 + 4 * half:12 + 4 * half], stat[:, 4 * half:4 * half + 4],
                               ACT.Sqrt).then_inc(s_x2rt, 1)
            for i in range(2 * KC):
                half, c = i // KC, i % KC
                act.wait_ge(s_x2T, i + 1)
                act.activation(hn_hi[:, c, half * HN:(half + 1) * HN], ps[:, i % 4, :], ACT.Copy,
                               scale=vec[:, V_N2 + c:V_N2 + c + 1]).then_inc(s_hnhi, 1)

            def hidden(g, par, first):
                for s in range(2):
                    act.wait_ge(s_up, 2 * g + s + 1)
                    if not first:
                        act.wait_ge(s_rsq, 2 * g + s - 1)
                    act.activation(relu_t[s][:, :], bank(2 * s, 2), ACT.Relu).then_inc(s_relu, 1)
                    if not (isinstance(g, int) and g < 2):
                        act.wait_ge(s_dn, 16 * g - 16)
                    act.wait_ge(s_rsq, 2 * g + s + 1)
                    act.activation(a_hi[par][:, s, :], relu_sq[s][:, :], ACT.Copy).then_inc(s_ahi, 1)

            hidden(0, 0, True)
            hidden(1, 1, False)
            with act.Fori(1, NFG // 2) as i:
                for par in range(2):
                    hidden(2 * i + par, par, False)

        @block.vector
        def _(dve):
            mine = Count(dve, s_dve)

            def step(instruction):
                mine.add(instruction)
                mine.wait()

            dve.wait_ge(s_tab, 1)
            dve.tensor_copy(vec[:, :], ps[:, 7, 0:N_VEC]).then_inc(s_tabr, 1)
            dve.tensor_copy(cw[:, :, :], ps[:, 6, 0:256].rearrange("p (c j) -> p c j", c=KC)).then_inc(s_tabr, 1)
            step(dve.tensor_scalar(stat[:, 32:48], sink[:, :], -1.0, None, ALU.mult))

            def row_norm(src, dst, half, summed, ms, root, done):
                a, b = 4 * half, 4 * half + 4
                dve.wait_ge(summed, b)
                dve.tensor_scalar(stat[:, a:b], stat[:, a:b], 1.0 / D, EPS, ALU.mult, ALU.add).then_inc(ms, 1)
                dve.wait_ge(root, half + 1)
                step(dve.reciprocal(stat[:, 8 + a:8 + b], stat[:, 8 + a:8 + b]))
                for t in range(a, b):
                    dve.tensor_scalar(dst[:, t, :], src[:, t, :], stat[:, 8 + t:9 + t], None, ALU.mult).then_inc(done, 1)

            def lo_part(i, dst, scale, hi, hi_sem, done):
                half, c = i // KC, i % KC
                cols = slice(half * HN, (half + 1) * HN)
                dve.wait_ge(hi_sem, i + 1)
                dve.scalar_tensor_tensor(out=dst[:, c, cols], in0=ps[:, i % 4, :], scalar=vec[:, scale + c:scale + c + 1],
                                         in1=hi[:, c, cols].bitcast(F32), op0=ALU.mult, op1=ALU.subtract).then_inc(done, 1)

            for half in range(2):
                row_norm(x_tok, x_tok, half, s_xss, s_xms, s_xrt, s_xn)
            for i in range(2 * KC):
                lo_part(i, h_lo, V_N1, h_hi, s_hhi, s_h)

            def qkv_sum(j):
                g, kp, t = j // 32, j // 8 % 4, j % 8
                dst, src = kv_tok[:, t, :], ps[:, j % 4, :]
                if g:
                    dst = q_tok[:, t, (g - 1) * HN:g * HN].rearrange("x (j s d) -> x s j d", j=GRP, s=2)
                    src = src.rearrange("x (s j d) -> x s j d", j=GRP, s=2)
                dve.wait_ge(s_qkvp, j + 1)
                if kp == 0:
                    dve.tensor_copy(dst, src).then_inc(s_qkvs, 1)
                else:
                    dve.wait_ge(s_qkvs, j - 7)
                    dve.tensor_tensor(dst, src, dst, ALU.add).then_inc(s_qkvs, 1)

            def head_steps(i, tok, c0, heads, gain):
                v = tok[:, :, c0:c0 + heads * HD].rearrange("p t (h d) -> p t h d", d=HD)
                rs = head_rs[:, :, 0:heads]

                def sums():
                    for th in range(2):
                        dve.wait_ge(s_sq, 2 * i + th + 1)
                        sq = squares[:, :, 0:heads * HD].rearrange("p t (h d) -> p t h d", d=HD)
                        ins = dve.tensor_reduce(head_ss[:, 4 * th:4 * th + 4, 0:heads], sq, AX.X, ALU.add)
                        ins.then_inc(s_ss, 1)
                    dve.wait_ge(s_ss, 2 * i + 2)
                    dve.tensor_scalar(head_ss[:, :, 0:heads], head_ss[:, :, 0:heads], 1.0 / HD, EPS,
                                      ALU.mult, ALU.add).then_inc(s_ms, 1)

                def norm():
                    dve.wait_ge(s_rt, i + 1)
                    step(dve.reciprocal(rs, rs))
                    for t in range(TT):
                        ins = dve.tensor_tensor(v[:, t], v[:, t], rs[:, t].unsqueeze(2).broadcast_to([P, heads, HD]), ALU.mult)
                    step(ins)

                def gains():
                    for t in range(TT):
                        ins = dve.tensor_tensor(v[:, t], v[:, t], gain[:, :].unsqueeze(1).broadcast_to([P, heads, HD]), ALU.mult)
                    step(ins)

                def rotate():
                    t1, t2 = v[:, :, :, 0:HALF], v[:, :, :, HALF:ROT]
                    cos, sin = (a[:, :, :].unsqueeze(2).broadcast_to([P, TT, heads, HALF]) for a in (cos_sb, sin_sb))
                    r = [x[:, :, 0:heads, :] for x in rope_tmp]
                    dve.tensor_tensor(r[0], t1, cos, ALU.mult)
                    dve.tensor_tensor(r[1], t2, sin, ALU.mult)
                    dve.tensor_tensor(r[2], t2, cos, ALU.mult)
                    step(dve.tensor_tensor(r[3], t1, sin, ALU.mult))
                    dve.tensor_tensor(t1, r[0], r[1], ALU.subtract)
                    dve.tensor_tensor(t2, r[2], r[3], ALU.add).then_inc(s_qk, 1)

                return [sums, norm, gains, rotate]

            k_steps = head_steps(0, kv_tok, 0, N_KV, gk)
            q_steps = [head_steps(1 + g, q_tok, g * HN, 8, gq) for g in range(2)]

            def values_lo():
                dve.wait_ge(s_vhi, 1)
                dve.tensor_tensor(v_lo[:, :, :], kv_tok[:, :, KV_W:2 * KV_W], v_hi[:, :, :].bitcast(F32),
                                  ALU.subtract).then_inc(s_v, 1)

            for g in range(3):
                pieces = [[], k_steps, q_steps[0]][g]
                for kp in range(4):
                    for t in range(TT):
                        qkv_sum(32 * g + 8 * kp + t)
                    if pieces:
                        pieces[kp]()
                    if g == 1 and kp == 0:
                        values_lo()
            for piece in q_steps[1]:
                piece()

            def mask_scores(G):
                b, kv, i = G // N_KV, G % N_KV, G % 2
                lo = P if b == 0 else 0
                dve.wait_ge(s_sc, G + 1)
                if G >= 2:
                    dve.wait_ge(s_pT, G - 1)
                for j in range(GRP):
                    c0 = (j % 2) * 256
                    ins = dve.tensor_tensor_reduce(probs[i][:, j, lo:], ps[:, 4 + j // 2, c0 + lo:c0 + 256], mask[:, lo:],
                                                   HD ** -0.5, NEG, ALU.add, ALU.max, stat[:, 24 + 4 * i + j:25 + 4 * i + j])
                step(ins)
                neg = stat[:, 4 * i:4 * i + 4]
                sinks_neg = stat[:, 32 + GRP * kv:36 + GRP * kv]
                step(dve.scalar_tensor_tensor(out=neg, in0=stat[:, 24 + 4 * i:28 + 4 * i], scalar=-1.0, in1=sinks_neg,
                                              op0=ALU.mult, op1=ALU.min))
                dve.tensor_tensor(stat[:, 16 + 4 * i:20 + 4 * i], neg, sinks_neg, ALU.subtract).then_inc(s_mx, 1)

            def normalise(G):
                i = G % 2
                lo = P if G < N_KV else 0
                total = stat[:, 8 + 4 * i:12 + 4 * i]
                dve.wait_ge(s_exp, G + 1)
                step(dve.tensor_tensor(total, total, stat[:, 16 + 4 * i:20 + 4 * i], ALU.add))
                step(dve.reciprocal(total, total))
                pr = probs[i][:, :, lo:]
                dve.tensor_tensor(pr, pr, total.unsqueeze(2).broadcast_to([P, GRP, 2 * P - lo]), ALU.mult).then_inc(s_pn, 1)

            def pt_low(G):
                lo = 1 if G < N_KV else 0
                dve.wait_ge(s_pThi, G + 1)
                dve.tensor_tensor(pt_lo[:, lo:, :], ps[:, 6 + lo:8, :], pt_hi[:, lo:, :].bitcast(F32),
                                  ALU.subtract).then_inc(s_pTr, 1)

            NG = TT * N_KV
            for G in range(NG + 1):
                if G < NG:
                    mask_scores(G)
                if G >= 1:
                    normalise(G - 1)
                    pt_low(G - 1)

            for t in range(TT):
                dve.wait_ge(s_ohi, t + 1)
                dve.tensor_tensor(o_lo[:, t, :, :], o_raw[:, t, :, :], o_hi[:, t, :, :].bitcast(F32),
                                  ALU.subtract).then_inc(s_o, 1)
            for f in range(KC):
                dve.wait_ge(s_gas, f + 1)
                dve.wait_ge(s_ya, f + 1)
                dve.tensor_tensor(ga[:, f, :], bank(2 * (f % 2), 2), ga[:, f, :], ALU.mult).then_inc(s_ma, 1)

            for u in range(2):
                dve.memset(glu[u][:, 0:PAD], 0.0).then_inc(s_gfree, 1)
            n0 = mine.n
            with dve.Fori(0, KC // 2) as i:
                mine.n = n0 + 2 * (TAPS - 1) * i
                for u in range(2):
                    c = 2 * i + u
                    tap = cw[:, bass.ds(c, 1), :].rearrange("p c j -> p (c j)")
                    y_c = y[:, bass.ds(c, 1), :].rearrange("p c n -> p (c n)")
                    dve.wait_ge(s_ca, c + 1)
                    dve.wait_ge(s_cs, c + 1)
                    dve.tensor_tensor(glu[u][:, PAD:PAD + S], bank(0, 2), glu[u][:, PAD:PAD + S], ALU.mult).then_inc(s_glu, 1)
                    dve.wait_ge(s_glu, c + 1)
                    step(dve.tensor_scalar(y_c, glu[u][:, 0:S], tap[:, 0:1], vec[:, bass.ds(V_CB + c, 1)],
                                           ALU.mult, ALU.add))
                    for j in range(1, TAPS):
                        ins = dve.scalar_tensor_tensor(out=y_c, in0=glu[u][:, j:j + S], scalar=tap[:, j:j + 1],
                                                       in1=y_c, op0=ALU.mult, op1=ALU.add)
                        if j < TAPS - 1:
                            step(ins)
                    ins.then_inc(s_gfree, 1)
            mine.n = n0 + 2 * (TAPS - 1) * (KC // 2)

            dve.wait_ge(s_mean, 1)
            for c in range(KC):
                dve.tensor_tensor(y[:, c, :], y[:, c, :], bank(0, 2), ALU.subtract).then_inc(s_yc, 1)
            dve.wait_ge(s_ysu, KC)
            dve.tensor_scalar(ln_rs[:, :], bank(2, 2), EPS, None, ALU.add).then_inc(s_var, 1)
            dve.wait_ge(s_std, 1)
            step(dve.reciprocal(ln_rs[:, :], ln_rs[:, :]))

            def scale_row(c):
                dve.tensor_tensor(y[:, c, :], y[:, c, :], ln_rs[:, :], ALU.mult).then_inc(s_z, 1)

            scale_row(0)
            scale_row(1)
            for c in range(KC):
                dve.wait_ge(s_sw, c + 1)
                dve.tensor_tensor(y[:, c, :], y[:, c, :], sig[c % 2][:, :], ALU.mult).then_inc(s_c, 1)
                if c + 2 < KC:
                    scale_row(c + 2)
                if c:
                    dve.wait_ge(s_chi, c)
                    dve.tensor_tensor(c_lo[:, c - 1, :], y[:, c - 1, :], c_hi[:, c - 1, :].bitcast(F32),
                                      ALU.subtract).then_inc(s_clo, 1)
            dve.wait_ge(s_chi, KC)
            dve.tensor_tensor(c_lo[:, KC - 1, :], y[:, KC - 1, :], c_hi[:, KC - 1, :].bitcast(F32),
                              ALU.subtract).then_inc(s_clo, 1)

            for f in range(KC):
                dve.wait_ge(s_yb, f + 1)
                dve.tensor_tensor(gb[:, f, :], bank(2 * (f % 2), 2), gb[:, f, :], ALU.mult).then_inc(s_mb, 1)
                dve.wait_ge(s_mb, f + 1)
                dve.tensor_tensor(gb[:, f, :], gb[:, f, :], ga[:, f, :], ALU.add).then_inc(s_ms2, 1)
                dve.wait_ge(s_mhi, f + 1)
                dve.tensor_tensor(m_lo[:, f, :], gb[:, f, :], m_hi[:, f, :].bitcast(F32), ALU.subtract).then_inc(s_m, 1)

            dve.wait_ge(s_x2in, 16 * TT)
            for j in range(64):
                g, t = j // 32, j % TT
                dve.wait_ge(s_op, j + 1)
                if j % 32 >= 8:
                    dve.wait_ge(s_os, j - 7)
                dst = x2[:, t, g * HN:(g + 1) * HN]
                dve.tensor_tensor(dst, ps[:, t % 4, :], dst, ALU.add).then_inc(s_os, 1)
            for half in range(2):
                row_norm(x2, xn2, half, s_x2ss, s_x2ms, s_x2rt, s_x2n)
            for i in range(2 * KC):
                lo_part(i, hn_lo, V_N2, hn_hi, s_hnhi, s_hn)

            def hidden(g, par, first):
                for s in range(2):
                    dve.wait_ge(s_relu, 2 * g + s + 1)
                    if not first:
                        dve.wait_ge(s_a, 2 * g + s - 1)
                    dve.tensor_tensor(relu_sq[s][:, :], relu_t[s][:, :], relu_t[s][:, :], ALU.mult).then_inc(s_rsq, 1)
                    dve.wait_ge(s_ahi, 2 * g + s + 1)
                    dve.tensor_tensor(a_lo[par][:, s, :], relu_sq[s][:, :], a_hi[par][:, s, :].bitcast(F32),
                                      ALU.subtract).then_inc(s_a, 1)

            def residual(g):
                for j in range(16):
                    s, t = j // 8, j % 8
                    dst = x2[:, t, s * HN:(s + 1) * HN]
                    dve.wait_ge(s_dn, 16 * g + j + 1)
                    if not (isinstance(g, int) and g == 0):
                        dve.wait_ge(s_ds, 16 * g + j - 15)
                    dve.tensor_tensor(dst, ps[:, 4 + t % 4, :], dst, ALU.add).then_inc(s_ds, 1)

            hidden(0, 0, True)
            hidden(1, 1, False)
            residual(0)
            with dve.Fori(0, (NFG - 2) // 2) as i:
                for par in range(2):
                    g = 2 * i + par + 1
                    hidden(g + 1, par, False)
                    residual(g)
            residual(NFG - 1)


INPUTS = ["x", "norm1_g", "w_in", "gate_b", "q_norm_g", "k_norm_g", "sinks", "w_attn_out", "conv_w", "conv_b",
          "conv_norm_g", "conv_norm_b", "w_conv_out", "w_out", "norm2_g", "w_up", "w_down"]


def kernel(**inputs):
    import concourse.bacc as bacc
    from concourse.bass_utils import run_bass_kernel_spmd

    nc = bacc.Bacc("TRN2", target_bir_lowering=False, num_devices=1)
    arrays, args = {}, []
    cos_t, sin_t = rope_tables()
    named = [(n, np.ascontiguousarray(inputs[n])) for n in INPUTS] + [("cos_t", cos_t), ("sin_t", sin_t)]
    for name, a in named:
        arrays[f"in_{name}"] = a
        args.append(nc.dram_tensor(f"in_{name}", a.shape, mybir.dt.from_np(a.dtype), kind="ExternalInput").ap())
    args.append(nc.dram_tensor("out_x", (1, S, D), F32, kind="ExternalOutput").ap())
    hybrid_block(nc, *args)
    return run_bass_kernel_spmd(nc, [arrays], core_ids=[0]).results[0]["out_x"]
```

```python
from contextlib import ExitStack

import numpy as np

import concourse.bass as bass
from concourse import mybir

F32 = mybir.dt.float32
F32R = mybir.dt.float32r
ALU = mybir.AluOpType
ACT = mybir.ActivationFunctionType
AX = mybir.AxisListType

P = 128
D = 1024
S = 1024
KC = D // P
TT = S // P
HN = 512
N_Q, N_KV, HD = 16, 4, 64
GRP = N_Q // N_KV
ROT = HD // 4
HALF = ROT // 2
THETA = 500000.0
Q_W = N_Q * HD
KV_W = N_KV * HD
TAPS = 31
PAD = TAPS - 1
FF = 4 * D
EPS = 1e-6
COL_A = Q_W + 2 * KV_W
COL_G = COL_A + D
COL_GATE = COL_A + 2 * D
COL_GATE2 = COL_GATE + D
SLOTS = 4
FFG = 256
NFG = FF // FFG
NEG = -1e30

MIDDLE = ([("g", 0), ("a", 0)] + [("g", 1), ("a", 1), ("g", 2), ("a", 2), ("A", 0), ("A", 1)]
          + [("g", 3), ("a", 3), ("A", 2), ("A", 3), ("A", 4), ("g", 4), ("a", 4), ("A", 5), ("A", 6), ("A", 7)]
          + [("g", 5), ("a", 5), ("Y", 0), ("Y", 1), ("g", 6), ("a", 6), ("Y", 2), ("Y", 3), ("Y", 4)]
          + [("g", 7), ("a", 7), ("Y", 5), ("Y", 6), ("Y", 7)] + [("B", f) for f in range(8)])
N_QKV, N_COVER, N_ATT, N_YB, N_OUT, N_MLP = 12, 2, 6, 8, 8, 4 * NFG
T_MID = N_QKV
T_ATT = T_MID + N_COVER
T_LATE = T_ATT + N_ATT
T_YB = T_MID + len(MIDDLE)
T_GB = T_YB - KC
T_OUT = T_YB + N_YB
T_MLP = T_OUT + N_OUT
N_TILES = T_MLP + N_MLP
CSTEPS = 2 * TAPS
CONV_SPANS = [(0, 10), (10, 21), (21, TT * N_KV)]
EARLY = len(CONV_SPANS)

V_N1, V_GA, V_GB, V_CB, V_CG, V_CNB, V_N2 = 0, 8, 16, 24, 32, 40, 48
N_VEC = 56


class Count:

    def __init__(self, engine, sem):
        self.engine, self.sem, self.n = engine, sem, 0

    def add(self, instruction):
        instruction.then_inc(self.sem, 1)
        self.n = self.n + 1
        return self.n

    def wait(self, n=None):
        self.engine.wait_ge(self.sem, self.n if n is None else n)


def rope_tables():
    power = np.power(np.float32(THETA), np.arange(0, ROT, 2, dtype=np.float32) / np.float32(ROT))
    angle = np.arange(S, dtype=np.float32)[:, None] * (np.float32(1.0) / power.astype(np.float32))[None, :]
    return np.cos(angle).astype(np.float32), np.sin(angle).astype(np.float32)


def hybrid_block(nc, x, norm1_g, w_in, gate_b, q_norm_g, k_norm_g, sinks, w_attn_out, conv_w, conv_b,
                 conv_norm_g, conv_norm_b, w_conv_out, w_out, norm2_g, w_up, w_down, cos_t, sin_t, out):
    x_tiles = x[0].rearrange("(t p) d -> t p d", p=P)
    out_tiles = out[0].rearrange("(t p) d -> t p d", p=P)
    base = 16896
    KB = 1024

    with ExitStack() as ctx:
        def sb(name, kb, shape, dt=F32):
            return nc.alloc_sbuf_tensor_at(name, shape, dt, offset=base + int(kb * KB))

        def sem(name):
            return ctx.enter_context(nc.semaphore(name))

        h_hi = sb("h_hi", 0, [P, KC, S], F32R)
        h_lo = sb("h_lo", 32, [P, KC, S], F32R)
        ma = sb("ma", 0, [P, KC, S])
        m_hi = sb("m_hi", 32, [P, KC, S], F32R)
        hn_hi = sb("hn_hi", 0, [P, KC, S], F32R)
        hn_lo = sb("hn_lo", 32, [P, KC, S], F32R)
        x_tok = sb("x_tok", 64, [P, TT, D])
        q_tok = sb("q_tok", 64, [P, TT, Q_W])
        o_raw = sb("o_raw", 64, [P, TT, KC, P])
        o_lo = sb("o_lo", 64, [P, TT, KC, P], F32R)
        y = sb("y", 64, [P, KC, S])
        c_lo = sb("c_lo", 64, [P, KC, S], F32R)
        x2 = sb("x2", 64, [P, TT, D])
        kv_tok = sb("kv_tok", 96, [P, TT, 2 * KV_W])
        cos_sb = sb("cos_sb", 112, [P, TT, HALF])
        sin_sb = sb("sin_sb", 112.25, [P, TT, HALF])
        gq = sb("gq", 112.5, [P, HD])
        gk = sb("gk", 112.75, [P, HD])
        ga = sb("ga", 96, [P, KC, S])
        c_hi = sb("c_hi", 96, [P, KC, S], F32R)
        xr = sb("xr", 96, [P, TT, D])
        GLU_W = PAD + S
        glu_kb = GLU_W * 4 / KB
        y_early = [sb(f"y_early{c}", 107.75 + 4 * c, [P, S]) for c in range(EARLY)]
        glu_early = [sb(f"glu_early{i}", 119.75 + (GLU_W * 4 + 8) * i / KB, [P, GLU_W]) for i in range(2)]
        xn2 = sb("xn2", 96, [P, TT, D])
        a_hi = [sb(f"a_hi{i}", 96 + 16 * i, [P, 2, S], F32R) for i in range(2)]
        a_lo = [sb(f"a_lo{i}", 104 + 16 * i, [P, 2, S], F32R) for i in range(2)]
        w_hi = [sb(f"w_hi{i}", 128 + 8 * i, [P, D], F32R) for i in range(SLOTS)]
        w_raw = [sb(f"w_raw{i}", 132 + 8 * i, [P, D]) for i in range(SLOTS)]
        w_lo = [sb(f"w_lo{i}", 132 + 8 * i, [P, D], F32R) for i in range(SLOTS)]
        junk = sb("junk", 160, [P, D])
        cw_rows = sb("cw_rows", 164, [32, D])
        vec_rows = sb("vec_rows", 168, [N_VEC, P])
        k_t = sb("k_t", 160, [P, 2, S])
        v_hi = sb("v_hi", 168, [P, TT, KV_W], F32R)
        v_lo = sb("v_lo", 176, [P, TT, KV_W], F32R)
        squares = sb("squares", 184, [P, 4, HN])
        rope_tmp = [sb(f"rope_tmp{i}", 192 + 2 * i, [P, TT, 8, HALF]) for i in range(4)]
        head_ss = sb("head_ss", 200, [P, TT, 8])
        head_rs = sb("head_rs", 200.25, [P, TT, 8])
        probs = [sb(f"probs{i}", 184 + 4 * i, [P, GRP, 2 * P]) for i in range(2)]
        pt_hi = sb("pt_hi", 192, [P, 2, HN], F32R)
        pt_lo = sb("pt_lo", 196, [P, 2, HN], F32R)
        q_t = [sb(f"q_t{i}", 200 + 2 * i, [P, HN]) for i in range(2)]
        mask = sb("mask", 204, [P, 2 * P])
        o_hi = sb("o_hi", 160, [P, TT, KC, P], F32R)
        gb = sb("gb", 160, [P, KC, S])
        m_lo = sb("m_lo", 160, [P, KC, S], F32R)
        glu_late = sb("glu_late", 192, [P, GLU_W])
        y_late = [sb(f"y_late{i}", 196.25 + 4 * i, [P, S]) for i in range(2)]
        y_sum = sb("y_sum", 192, [P, S])
        ln_rs = sb("ln_rs", 192, [P, S])
        sq_y = [sb(f"sq_y{i}", 196 + 4 * i, [P, S]) for i in range(2)]
        sig = [sb(f"sig{i}", 196 + 4 * i, [P, S]) for i in range(2)]
        junk2 = sb("junk2", 192, [P, D])
        relu_t = [sb(f"relu_t{i}", 160 + 4 * i, [P, S]) for i in range(2)]
        relu_sq = [sb(f"relu_sq{i}", 168 + 4 * i, [P, S]) for i in range(2)]
        small = 205 * KB
        ident = sb("ident", small / KB, [P, P])
        mean_w = sb("mean_w", (small + 512) / KB, [P, P])
        vec = sb("vec", (small + 1024) / KB, [P, N_VEC])
        cw = sb("cw", (small + 1248) / KB, [P, KC, 32])
        sink = sb("sink", (small + 2272) / KB, [P, N_Q])
        stat = sb("stat", (small + 2336) / KB, [P, 48])

        y_dram = nc.dram_tensor("y_spilled", (KC, P, S), F32).ap()
        ma_dram = nc.dram_tensor("ma_spilled", (KC, P, S), F32).ap()

        def glu_of(c):
            return glu_early[c % 2] if c < EARLY else glu_late

        def y_of(c):
            return y_early[c] if c < EARLY else y_late[c % 2]

        ps = ctx.enter_context(nc.psum_tensor("ps", [P, 8, HN], F32))

        def bank(b, n=1):
            return ps[:, b:b + n, :].rearrange("p b n -> p (b n)")

        s_x = [sem(f"x_landed{t}") for t in range(TT)]
        s_const = sem("constants_landed")
        s_cwzero = sem("conv_taps_zeroed")
        s_ident = sem("identity_built")
        s_landed = [sem(f"weights_landed{i}") for i in range(SLOTS)]
        s_seen = sem("weights_seen")
        s_hi = sem("weights_hi_split")
        s_split = sem("weights_split")
        s_begun = sem("tiles_begun")
        s_dve = sem("vector_steps")
        s_tab = sem("tables_transposed")
        s_tabr = sem("tables_ready")
        s_xss = sem("x_squares_summed")
        s_xms = sem("x_mean_square")
        s_xrt = sem("x_root")
        s_xn = sem("x_normalised")
        s_xT = sem("x_transposed")
        s_hhi = sem("h_hi_ready")
        s_h = sem("h_ready")
        s_qkvp = sem("qkv_partial")
        s_qkvs = sem("qkv_summed")
        s_sq = sem("head_squares")
        s_ss = sem("head_squares_summed")
        s_ms = sem("head_mean_square")
        s_rt = sem("head_root")
        s_qk = sem("heads_ready")
        s_vhi = sem("v_hi_ready")
        s_v = sem("v_ready")
        s_kT = sem("k_transposed")
        s_kTr = sem("k_t_ready")
        s_qT = sem("q_transposed")
        s_qTr = sem("q_t_ready")
        s_sc = sem("scores")
        s_mx = sem("scores_masked")
        s_exp = sem("exps")
        s_rl = sem("totals_inverted")
        s_pn = sem("probs_normalised")
        s_pT = sem("probs_transposed")
        s_pThi = sem("pt_hi_ready")
        s_pTr = sem("pt_ready")
        s_pv = sem("values_mixed")
        s_oe = sem("o_stored")
        s_ga = sem("gate_a_logits")
        s_gas = sem("gate_a_ready")
        s_ohi = sem("o_hi_ready")
        s_o = sem("o_ready")
        s_ya = sem("y_attn")
        s_ma = sem("attn_merged")
        s_ca = sem("conv_a")
        s_cg = sem("conv_gate")
        s_cs = sem("conv_sigmoid")
        s_glu = sem("glu_ready")
        s_cv = sem("conv_steps")
        s_sp = [sem(f"y_spilled{c}") for c in range(KC)]
        s_masp = sem("attn_merged_spilled")
        s_mal = sem("attn_merged_reloaded")
        s_yin = [sem(f"y_reloaded{c}") for c in range(KC)]
        s_ysum = sem("y_summed")
        s_gbl = sem("gate_b_logits")
        s_gb = sem("gate_b_ready")
        s_mean = sem("mean_ready")
        s_yc = sem("centred")
        s_ysq = sem("centred_squares")
        s_ysu = sem("squares_added")
        s_vsum = sem("variance_summed")
        s_var = sem("variance_ready")
        s_std = sem("std_ready")
        s_z = sem("ln_scaled")
        s_sw = sem("ln_sigmoid")
        s_c = sem("conv_out_ready")
        s_chi = sem("c_hi_ready")
        s_clo = sem("c_ready")
        s_yb = sem("y_conv")
        s_mb = sem("y_conv_read")
        s_ms2 = sem("merged")
        s_mhi = sem("m_hi_ready")
        s_m = sem("m_ready")
        s_x2in = sem("x_reloaded")
        s_xa = sem("residual_added")
        s_op = sem("out_partial")
        s_os = sem("out_summed")
        s_x2ss = sem("x2_squares_summed")
        s_x2ms = sem("x2_mean_square")
        s_x2rt = sem("x2_root")
        s_x2n = sem("x2_normalised")
        s_x2T = sem("x2_transposed")
        s_hnhi = sem("hn_hi_ready")
        s_hn = sem("hn_ready")
        s_up = sem("up_done")
        s_relu = sem("relu_done")
        s_rsq = sem("relu_squared")
        s_ahi = sem("a_hi_ready")
        s_a = sem("a_ready")
        s_dn = sem("down_partial")
        s_ds = sem("down_summed")
        s_out = sem("output_stored")

        block = ctx.enter_context(nc.Block())

        def column_tile(w, c0):
            return w.rearrange("(k p) n -> p k n", p=P)[:, :, bass.ds(c0, P)]

        def row_tile(w, k0, c0):
            return w[bass.ds(k0, 2 * P), bass.ds(c0, HN)].rearrange("(k p) n -> p k n", p=P)

        @block.sync
        def _(sp):
            for t in range(TT):
                sp.dma_start(x_tok[:, t, :], x_tiles[t]).then_inc(s_x[t], 16)

            def load(n, slot, src, wait=True):
                if wait:
                    sp.wait_ge(s_begun, n - SLOTS + 2)
                k = src.shape[1]
                sp.dma_start(w_raw[slot][:, :].rearrange("p (k n) -> p k n", k=k), src).then_inc(s_landed[slot], 16)

            for g, c0 in enumerate((0, HN, Q_W)):
                for kp in range(4):
                    load(4 * g + kp, kp, row_tile(w_in[0], 2 * P * kp, c0), wait=g > 0)
            for i, (kind, f) in enumerate(MIDDLE):
                n = T_MID + i
                if n == T_GB + 3 or n == T_GB + 4:
                    sp.wait_ge(s_begun, T_GB + 1)
                    for c in range(KC - 1) if n == T_GB + 3 else [KC - 1]:
                        sp.wait_ge(s_sp[c], 16)
                        sp.dma_start(y[:, c, :], y_dram[c]).then_inc(s_yin[c], 16)
                w, c0 = {"g": (w_in, COL_G), "a": (w_in, COL_A), "A": (w_in, COL_GATE), "B": (w_in, COL_GATE2),
                         "Y": (w_attn_out, 0)}[kind]
                load(n, n % SLOTS, column_tile(w[0], c0 + f * P))
            for f in range(N_YB):
                n = T_YB + f
                if f == 3:
                    sp.wait_ge(s_begun, T_YB + 1)
                    sp.wait_ge(s_masp, 16 * KC)
                    for c in range(KC):
                        sp.dma_start(ma[:, c, :], ma_dram[c]).then_inc(s_mal, 16)
                load(n, n % SLOTS, column_tile(w_conv_out[0], f * P))
            for j in range(N_OUT):
                n = T_OUT + j
                if j == 3:
                    sp.wait_ge(s_begun, T_OUT + 1)
                    for t in range(TT):
                        sp.dma_start(xr[:, t, :], x_tiles[t]).then_inc(s_x2in, 16)
                load(n, n % SLOTS, row_tile(w_out[0], 2 * P * (j % 4), (j // 4) * HN))

            for s in range(2):
                load(T_MLP + s, s, column_tile(w_up[0], s * P))
            with sp.Fori(0, NFG - 1) as g:
                for s in range(2):
                    load(T_MLP + 2 + 4 * g + s, 2 + s, column_tile(w_up[0], (2 * g + 2 + s) * P))
                for s in range(2):
                    load(T_MLP + 4 + 4 * g + s, s, row_tile(w_down[0], g * FFG, s * HN))
            for s in range(2):
                load(N_TILES - 2 + s, 2 + s, row_tile(w_down[0], FF - FFG, s * HN))
            for t in range(TT):
                sp.wait_ge(s_ds, 16 * (NFG - 1) + 8 + t + 1)
                sp.dma_start(out_tiles[t], x2[:, t, :]).then_inc(s_out, 16)
            sp.wait_ge(s_out, 16 * TT)

        @block.gpsimd
        def _(pool):
            pool.memset(cw_rows[:, :], 0.0).then_inc(s_cwzero, 1)
            pool.memset(ident[:, :], 0.0).then_inc(s_ident, 1)
            pool.memset(mean_w[:, :], 1.0 / D).then_inc(s_ident, 1)
            pool.memset(mask[:, :], 0.0).then_inc(s_ident, 1)
            pool.wait_ge(s_ident, 3)
            pool.affine_select(out=ident[:, :], in_=ident[:, :], compare_op=ALU.not_equal, fill=1.0,
                               base=0, pattern=[[-1, P]], channel_multiplier=1).then_inc(s_ident, 1)
            pool.affine_select(out=mask[:, 0:P], in_=mask[:, 0:P], compare_op=ALU.is_gt, fill=NEG,
                               base=0, pattern=[[1, P]], channel_multiplier=-1).then_inc(s_ident, 1)
            pool.affine_select(out=mask[:, P:2 * P], in_=mask[:, P:2 * P], compare_op=ALU.is_ge, fill=NEG,
                               base=0, pattern=[[-1, P]], channel_multiplier=1).then_inc(s_ident, 1)
            with pool.Fori(0, N_TILES // SLOTS) as i:
                for s in range(SLOTS):
                    pool.wait_ge(s_landed[s], 16 * i + 16)
                    pool.sem_inc(s_seen, 1)
                    pool.tensor_copy(w_hi[s][:, :], w_raw[s][:, :]).then_inc(s_hi, 1)
                    pool.wait_ge(s_hi, SLOTS * i + s + 1)
                    pool.tensor_tensor(w_lo[s][:, :], w_raw[s][:, :], w_hi[s][:, :].bitcast(F32),
                                       ALU.subtract).then_inc(s_split, 1)

        @block.tensor
        def _(pe):
            def column_product(n, slot, b, rhs_hi, rhs_lo, ks=range(KC)):
                pe.wait_ge(s_split, n + 1)
                wh = w_hi[slot][:, :].rearrange("p (k m) -> p k m", k=KC)
                wl = w_lo[slot][:, :].rearrange("p (k m) -> p k m", k=KC)
                for k in ks:
                    first, last = k == 0, k == KC - 1
                    for h in range(2):
                        o = ps[:, b + h, :]
                        mm = pe.matmul(o, wh[:, k, :], rhs_hi(k, h), start=first, stop=False)
                        if first and h == 0:
                            mm.then_inc(s_begun, 1)
                        pe.matmul(o, wh[:, k, :], rhs_lo(k, h), start=False, stop=False)
                    for h in range(2):
                        o = ps[:, b + h, :]
                        mm = pe.matmul(o, wl[:, k, :], rhs_hi(k, h), start=False, stop=last)
                return mm

            def row_product(b, lhs_hi, lhs_lo, slot, begins):
                wh = w_hi[slot][:, :].rearrange("p (k n) -> p k n", k=2)
                wl = w_lo[slot][:, :].rearrange("p (k n) -> p k n", k=2)
                for k in range(2):
                    mm = pe.matmul(ps[:, b, :], lhs_hi(k), wh[:, k, :], start=k == 0, stop=False)
                    if begins and k == 0:
                        mm.then_inc(s_begun, 1)
                    pe.matmul(ps[:, b, :], lhs_hi(k), wl[:, k, :], start=False, stop=False)
                    mm = pe.matmul(ps[:, b, :], lhs_lo(k), wh[:, k, :], start=False, stop=k == 1)
                return mm

            def halves(a):
                return lambda k, h: a[:, k, h * HN:(h + 1) * HN]

            pe.wait_ge(s_ident, 4)
            pe.wait_ge(s_const, 16 * 12)
            pe.transpose(ps[:, 7, 0:N_VEC], vec_rows[:, :], ident[0:N_VEC, 0:N_VEC])
            for c in range(KC):
                mm = pe.transpose(ps[:, 6, 32 * c:32 * c + 32], cw_rows[:, c * P:(c + 1) * P], ident[0:32, 0:32])
            mm.then_inc(s_tab, 1)

            def transposed(src, half, c, i, free, done, ready):
                b = 4 * half + c % 4
                if c >= 4:
                    pe.wait_ge(free, i - 3)
                if c == 0:
                    pe.wait_ge(ready, 4 * half + 4)
                for j in range(4):
                    mm = pe.transpose(ps[:, b, j * P:(j + 1) * P], src[:, 4 * half + j, c * P:(c + 1) * P],
                                      ident[:, :])
                mm.then_inc(done, 1)

            def h_transposes(half):
                for c in range(KC):
                    transposed(x_tok, half, c, half * KC + c, s_h, s_xT, s_xn)

            h_transposes(0)
            j = 0
            for g in range(3):
                for kp in range(4):
                    pe.wait_ge(s_split, 4 * g + kp + 1)
                    for t in range(TT):
                        if j == 0:
                            pe.wait_ge(s_h, KC)
                        if j == 4:
                            h_transposes(1)
                            pe.wait_ge(s_h, 2 * KC)
                        if j >= 4:
                            pe.wait_ge(s_qkvs, j - 3)
                        mm = row_product(j % 4, lambda k: h_hi[:, 2 * kp + k, t * P:(t + 1) * P],
                                         lambda k: h_lo[:, 2 * kp + k, t * P:(t + 1) * P], kp, t == 0)
                        mm.then_inc(s_qkvp, 1)
                        j += 1

            pair = {}
            for i, (kind, f) in enumerate(MIDDLE):
                if kind == "g" or N_COVER <= i < N_COVER + N_ATT:
                    pair[i] = 0
                elif kind == "a":
                    pair[i] = 4 if i < N_COVER else 2
                else:
                    pair[i] = 4 if sum(k in "AYB" for k, _ in MIDDLE[N_COVER + N_ATT:i]) % 2 == 0 else 6
            read_by = {"g": s_cs, "a": s_glu, "A": s_gas, "Y": s_ma, "B": s_gb}
            signals = {"g": s_cg, "a": s_ca, "A": s_ga, "Y": s_ya, "B": s_gbl}

            def middle_tile(i, part=None):
                kind, f = MIDDLE[i]
                rhs = (o_rhs(o_hi), o_rhs(o_lo)) if kind == "Y" else (halves(h_hi), halves(h_lo))
                before = [e for e in range(i) if pair[e] == pair[i]]
                if part in (None, 0) and before:
                    k, e = MIDDLE[before[-1]]
                    pe.wait_ge(read_by[k], e + 1)
                ks = range(KC) if part is None else range(2 * part, 2 * part + 2)
                mm = column_product(T_MID + i, (T_MID + i) % SLOTS, pair[i], *rhs, ks)
                if part in (None, 3):
                    mm.then_inc(signals[kind], 1)

            o_rhs = lambda o: (lambda k, h: o[:, 4 * h:4 * h + 4, k, :])

            def q_unit(u):
                b, p = u // 2, u % 2
                if u >= 1:
                    pe.wait_ge(s_qTr, u)
                for j in range(GRP):
                    c0 = (p * GRP + j) * P
                    mm = pe.transpose(ps[:, 3, j * P:(j + 1) * P], q_tok[:, b, c0:c0 + P], ident[:, :])
                mm.then_inc(s_qT, 1)

            def scores(G):
                b, kv = G // N_KV, G % N_KV
                p, s = kv // 2, kv % 2
                r = slice(64 * s, 64 * s + 64)
                pe.wait_ge(s_qTr, G // 2 + 1)
                if G:
                    pe.wait_ge(s_mx, G)
                else:
                    pe.wait_ge(s_glu, 1)
                keys = slice(max(b - 1, 0) * P, (b + 1) * P)
                lo = P if b == 0 else 0
                for j in range(GRP):
                    c0 = (j % 2) * 256
                    mm = pe.matmul(ps[:, 4 + j // 2, c0 + lo:c0 + 256], q_t[(G // 2) % 2][r, j * P:(j + 1) * P],
                                   k_t[r, p, keys], start=True, stop=True)
                mm.then_inc(s_sc, 1)

            def turn_probs(G):
                pe.wait_ge(s_pn, G + 1)
                if G:
                    pe.wait_ge(s_pTr, G)
                for hf in range(1 if G < N_KV else 0, 2):
                    for j in range(GRP):
                        mm = pe.transpose(ps[:, 6 + hf, j * P:(j + 1) * P],
                                          probs[G % 2][:, j, hf * P:(hf + 1) * P], ident[:, :])
                mm.then_inc(s_pT, 1)

            def mix_values(G):
                b, kv = G // N_KV, G % N_KV
                pe.wait_ge(s_pTr, G + 1)
                if G:
                    pe.wait_ge(s_oe, G)
                else:
                    pe.wait_ge(s_v, 1)
                hs = [1] if b == 0 else [0, 1]
                for hf in hs:
                    vh, vl = (v[:, b - 1 + hf, kv // 2 * P:(kv // 2 + 1) * P] for v in (v_hi, v_lo))
                    pe.matmul(ps[:, 2, :], vh, pt_hi[:, hf, :], start=hf == hs[0], stop=False)
                    pe.matmul(ps[:, 2, :], vh, pt_lo[:, hf, :], start=False, stop=False)
                    mm = pe.matmul(ps[:, 2, :], vl, pt_hi[:, hf, :], start=False, stop=hf == 1)
                mm.then_inc(s_pv, 1)

            pe.wait_ge(s_qkvs, 96)
            middle_tile(0)
            middle_tile(1)
            pe.wait_ge(s_qk, 3)
            for i, b in enumerate((6, 7, 2, 3)):
                for t in range(4):
                    mm = pe.transpose(ps[:, b, t * P:(t + 1) * P],
                                      kv_tok[:, 4 * (i % 2) + t, i // 2 * P:(i // 2 + 1) * P], ident[:, :])
                mm.then_inc(s_kT, 1)
            pe.wait_ge(s_kTr, 4)
            q_unit(0)
            q_unit(1)
            NG = TT * N_KV
            for G in range(NG + 2):
                if G < NG:
                    scores(G)
                    if G % 4 == 2 and G + 2 < NG:
                        q_unit((G + 2) // 2)
                    if G % 4 == 3 and G + 1 < NG:
                        q_unit((G + 1) // 2 + 1)
                    if G % 4 < 3:
                        q = 3 * (G // 4) + G % 4
                        middle_tile(N_COVER + q // 4, q % 4)
                if 2 <= G:
                    mix_values(G - 2)
                if 1 <= G <= NG:
                    turn_probs(G - 1)

            pe.wait_ge(s_mx, NG)
            pe.wait_ge(s_pTr, NG)
            pe.wait_ge(s_oe, NG)
            for i in range(N_COVER + N_ATT, len(MIDDLE) - KC):
                if MIDDLE[i] == ("Y", 0):
                    pe.wait_ge(s_o, TT)
                middle_tile(i)

            def channel_sum(b, src, ready, count, done):
                pe.wait_ge(ready, count)
                for h in range(2):
                    mm = pe.matmul(ps[:, b + h, :], mean_w[:, :], src[:, h * HN:(h + 1) * HN], start=True, stop=True)
                mm.then_inc(done, 1)

            for f in range(KC):
                middle_tile(len(MIDDLE) - KC + f)
                if f == 1:
                    channel_sum(0, y_sum, s_ysum, 1, s_mean)
                if f == 3:
                    channel_sum(2, y_sum, s_ysu, KC - 1, s_vsum)

            def eight_tiles(first_tile, rhs_hi, rhs_lo, done, free):
                with pe.Fori(0, 2) as i:
                    for s in range(SLOTS):
                        f = SLOTS * i + s
                        if s >= 2:
                            pe.wait_ge(free, f - 1)
                        mm = column_product(first_tile + f, s, 2 * (s % 2), rhs_hi, rhs_lo)
                        mm.then_inc(done, 1)
                    pe.wait_ge(free, SLOTS * i + SLOTS)

            pe.wait_ge(s_clo, KC)
            eight_tiles(T_YB, halves(c_hi), halves(c_lo), s_yb, s_mb)

            pe.wait_ge(s_m, KC)
            with pe.Fori(0, 2) as i:
                for kp in range(SLOTS):
                    pe.wait_ge(s_split, T_OUT + SLOTS * i + kp + 1)
                    for t in range(TT):
                        j = kp * TT + t
                        if j >= 4:
                            pe.wait_ge(s_os, 32 * i + j - 3)
                        mm = row_product(t % 4, lambda k: m_hi[:, 2 * kp + k, t * P:(t + 1) * P],
                                         lambda k: m_lo[:, 2 * kp + k, t * P:(t + 1) * P], kp, t == 0)
                        mm.then_inc(s_op, 1)
                pe.wait_ge(s_os, 32 * i + 32)

            for half in range(2):
                for c in range(KC):
                    transposed(xn2, half, c, half * KC + c, s_hn, s_x2T, s_x2n)
            pe.wait_ge(s_hn, 2 * KC)

            def up(g, n, slot0):
                for s in range(2):
                    if not (isinstance(g, int) and g == 0):
                        pe.wait_ge(s_relu, 2 * g + s - 1)
                    mm = column_product(n + s, slot0 + s, 2 * s, halves(hn_hi), halves(hn_lo))
                    mm.then_inc(s_up, 1)

            def down(g, parity, n, slot0):
                pe.wait_ge(s_a, 2 * g + 2)
                for s in range(2):
                    pe.wait_ge(s_split, n + s + 1)
                    for t in range(TT):
                        if not (isinstance(g, int) and g == 0 and s == 0 and t < 4):
                            pe.wait_ge(s_ds, 16 * g + 8 * s + t - 3)
                        mm = row_product(4 + t % 4, lambda k: a_hi[parity][:, k, t * P:(t + 1) * P],
                                         lambda k: a_lo[parity][:, k, t * P:(t + 1) * P], slot0 + s, t == 0)
                        mm.then_inc(s_dn, 1)

            up(0, T_MLP, 0)
            up(1, T_MLP + 2, 2)
            down(0, 0, T_MLP + 4, 0)
            with pe.Fori(0, (NFG - 2) // 2) as i:
                for par in range(2):
                    g = 2 * i + par + 1
                    up(g + 1, T_MLP + 2 + 4 * g, 2)
                    down(g, (par + 1) % 2, T_MLP + 4 + 4 * g, 0)
            down(NFG - 1, 1, N_TILES - 2, 2)

        @block.scalar
        def _(act):
            for r, v in ((V_N1, norm1_g[0]), (V_GA, gate_b[0]), (V_CB, conv_b[0]),
                         (V_CG, conv_norm_g[0]), (V_CNB, conv_norm_b[0]), (V_N2, norm2_g[0])):
                n = v.shape[0] // P
                act.dma_start(vec_rows[r:r + n, :], v.rearrange("(r c) -> r c", c=P)).then_inc(s_const, 16)
            act.wait_ge(s_cwzero, 1)
            act.dma_start(cw_rows[0:TAPS, :], conv_w[0]).then_inc(s_const, 16)
            act.dma_start(gq[:, :], q_norm_g.partition_broadcast(P)).then_inc(s_const, 16)
            act.dma_start(gk[:, :], k_norm_g.partition_broadcast(P)).then_inc(s_const, 16)
            act.dma_start(sink[:, :], sinks.partition_broadcast(P)).then_inc(s_const, 16)
            act.dma_start(cos_sb[:, :, :], cos_t.rearrange("(t p) h -> p t h", p=P)).then_inc(s_const, 16)
            act.dma_start(sin_sb[:, :, :], sin_t.rearrange("(t p) h -> p t h", p=P)).then_inc(s_const, 16)

            def row_squares(src, t, ss, done, trash=junk):
                act.activation(trash[:, :], src[:, t, :], ACT.Square, accum_out=ss).then_inc(done, 1)

            for half in range(2):
                for t in range(4 * half, 4 * half + 4):
                    act.wait_ge(s_x[t], 16)
                    if t:
                        act.wait_ge(s_xss, t)
                    row_squares(x_tok, t, stat[:, t:t + 1], s_xss)
                act.wait_ge(s_xms, half + 1)
                act.activation(stat[:, 8 + 4 * half:12 + 4 * half], stat[:, 4 * half:4 * half + 4],
                               ACT.Sqrt).then_inc(s_xrt, 1)

            act.wait_ge(s_tabr, 2)
            for i in range(2 * KC):
                half, c = i // KC, i % KC
                act.wait_ge(s_xT, i + 1)
                act.activation(h_hi[:, c, half * HN:(half + 1) * HN], ps[:, 4 * half + c % 4, :], ACT.Copy,
                               scale=vec[:, V_N1 + c:V_N1 + c + 1]).then_inc(s_hhi, 1)

            def head_squares(tok, c0, heads, summed, i0):
                for th in range(2):
                    act.wait_ge(s_qkvs, summed + 4 * th + 4)
                    if i0 + th:
                        act.wait_ge(s_ss, i0 + th)
                    act.activation(squares[:, :, 0:heads * HD], tok[:, 4 * th:4 * th + 4, c0:c0 + heads * HD],
                                   ACT.Square).then_inc(s_sq, 1)

            def head_root(i, heads):
                act.wait_ge(s_ms, i + 1)
                act.activation(head_rs[:, :, 0:heads], head_ss[:, :, 0:heads], ACT.Sqrt).then_inc(s_rt, 1)

            head_squares(q_tok, 0, 8, 24, 0)
            head_root(0, 8)
            head_squares(q_tok, HN, 8, 32 + 24, 2)
            head_root(1, 8)
            head_squares(kv_tok, 0, N_KV, 64 + 24, 4)
            head_root(2, N_KV)
            act.activation(v_hi[:, :, :], kv_tok[:, :, KV_W:2 * KV_W], ACT.Copy).then_inc(s_vhi, 1)

            def conv_gate(c):
                act.wait_ge(s_cg, c + 1)
                if c == 2 or c > EARLY:
                    act.wait_ge(s_cv, CSTEPS * (c - 2 if c == 2 else c - 1) + CSTEPS)
                act.activation(glu_of(c)[:, PAD:PAD + S], bank(0, 2), ACT.Sigmoid).then_inc(s_cs, 1)

            def store_gate_a(f, b):
                act.wait_ge(s_ga, f + 1)
                act.activation(ga[:, f, :], bank(b, 2), ACT.Sigmoid, bias=vec[:, V_GA + f:V_GA + f + 1]).then_inc(s_gas, 1)

            def store_gate_b(f, b):
                act.wait_ge(s_gbl, f + 1)
                act.activation(gb[:, f, :], bank(b, 2), ACT.Sigmoid, bias=vec[:, V_GB + f:V_GB + f + 1]).then_inc(s_gb, 1)

            conv_gate(0)
            for i, b in enumerate((6, 7, 2, 3)):
                act.wait_ge(s_kT, i + 1)
                act.activation(k_t[:, i // 2, (i % 2) * HN:(i % 2 + 1) * HN], ps[:, b, :], ACT.Copy).then_inc(s_kTr, 1)

            def q_store(u):
                act.wait_ge(s_qT, u + 1)
                if u >= 2:
                    act.wait_ge(s_sc, 2 * (u - 1))
                act.activation(q_t[u % 2][:, :], ps[:, 3, :], ACT.Copy).then_inc(s_qTr, 1)

            def exps(G):
                b, kv = G // N_KV, G % N_KV
                i = G % 2
                lo = P if b == 0 else 0
                act.wait_ge(s_mx, G + 1)
                for j in range(GRP):
                    pr = probs[i][:, j, lo:]
                    act.activation(pr, pr, ACT.Exp, bias=stat[:, 4 * i + j:4 * i + j + 1],
                                   accum_out=stat[:, 8 + 4 * i + j:9 + 4 * i + j])
                act.activation(stat[:, 16 + 4 * i:20 + 4 * i], stat[:, 16 + 4 * i:20 + 4 * i], ACT.Exp).then_inc(s_exp, 1)

            def normalise(G):
                i, lo = G % 2, P if G < N_KV else 0
                act.wait_ge(s_rl, G + 1)
                for j in range(GRP):
                    pr = probs[i][:, j, lo:]
                    ins = act.activation(pr, pr, ACT.Copy, scale=stat[:, 8 + 4 * i + j:9 + 4 * i + j])
                ins.then_inc(s_pn, 1)

            def store_o(G):
                b, kv = G // N_KV, G % N_KV
                act.wait_ge(s_pv, G + 1)
                r0 = 64 * (kv % 2)
                for r in range(2):
                    src = ps[r0:r0 + 64, 2, :].rearrange("p (jj s n) -> p jj s n", jj=2, s=2)[:, :, r, :]
                    ins = act.activation(o_raw[64 * r:64 * r + 64, b, 2 * kv:2 * kv + 2, :], src, ACT.Copy)
                ins.then_inc(s_oe, 1)

            def pt_store(G):
                lo = 1 if G < N_KV else 0
                act.wait_ge(s_pT, G + 1)
                if G:
                    act.wait_ge(s_pv, G)
                act.activation(pt_hi[:, lo:, :], ps[:, 6 + lo:8, :], ACT.Copy).then_inc(s_pThi, 1)

            NG = TT * N_KV
            q_store(0)
            q_store(1)
            for G in range(NG + 2):
                if G in (5, 15):
                    conv_gate(1 if G == 5 else 2)
                if G in (26, 31):
                    if G == 26:
                        act.wait_ge(s_v, 1)
                    store_gate_a(0 if G == 26 else 1, 0)
                if 1 <= G <= NG:
                    normalise(G - 1)
                if G < NG:
                    if G % 4 == 2 and G + 2 < NG:
                        q_store((G + 2) // 2)
                    if G % 4 == 3 and G + 1 < NG:
                        q_store((G + 1) // 2 + 1)
                    exps(G)
                if G >= 2:
                    store_o(G - 2)
                if 1 <= G <= NG:
                    pt_store(G - 1)

            def spill_y(c):
                act.wait_ge(s_cv, CSTEPS * c + CSTEPS)
                act.dma_start(y_dram[c], y_of(c)[:, :]).then_inc(s_sp[c], 16)

            def spill_ma(f):
                act.wait_ge(s_ma, f + 1)
                act.dma_start(ma_dram[f], ga[:, f, :]).then_inc(s_masp, 16)

            act.wait_ge(s_oe, NG)
            for t in range(TT):
                act.activation(o_hi[:, t, :, :], o_raw[:, t, :, :], ACT.Copy).then_inc(s_ohi, 1)
            for c in range(EARLY):
                spill_y(c)
            turn = 0
            for kind, f in MIDDLE[N_COVER + N_ATT:-KC]:
                b = 4 + 2 * (turn % 2)
                if kind == "g":
                    if f > EARLY:
                        spill_y(f - 1)
                    conv_gate(f)
                if kind == "A":
                    if f == 2:
                        for c in range(EARLY):
                            act.wait_ge(s_sp[c], 16)
                    store_gate_a(f, b)
                if kind == "Y":
                    spill_ma(f)
                turn += kind in "AY"
            store_gate_b(0, 4 + 2 * (turn % 2))
            spill_y(KC - 1)
            store_gate_b(1, 4 + 2 * ((turn + 1) % 2))

            for c in range(KC):
                act.wait_ge(s_yc, c + 1)
                if c >= 3:
                    act.wait_ge(s_ysu, c - 2)
                sq = y_sum if c == 0 else sq_y[c % 2]
                act.activation(sq[:, :], y[:, c, :], ACT.Square).then_inc(s_ysq, 1)
            for f in (2, 3):
                store_gate_b(f, 4 + 2 * ((turn + f) % 2))
            act.wait_ge(s_var, 1)
            act.activation(ln_rs[:, :], ln_rs[:, :], ACT.Sqrt).then_inc(s_std, 1)

            def c_store(c):
                act.wait_ge(s_c, c + 1)
                if c == 0:
                    act.wait_ge(s_masp, 16 * KC)
                act.activation(c_hi[:, c, :], y[:, c, :], ACT.Copy).then_inc(s_chi, 1)

            for c in range(KC):
                act.wait_ge(s_z, c + 1)
                if c >= 2:
                    act.wait_ge(s_c, c - 1)
                act.activation(sig[c % 2][:, :], y[:, c, :], ACT.Sigmoid,
                               bias=vec[:, V_CNB + c:V_CNB + c + 1]).then_inc(s_sw, 1)
                if c:
                    c_store(c - 1)
                if c in (2, 5):
                    f = 4 if c == 2 else 5
                    store_gate_b(f, 4 + 2 * ((turn + f) % 2))
            c_store(KC - 1)
            for f in (6, 7):
                store_gate_b(f, 4 + 2 * ((turn + f) % 2))

            for f in range(KC):
                act.wait_ge(s_ms2, f + 1)
                act.activation(m_hi[:, f, :], gb[:, f, :], ACT.Copy).then_inc(s_mhi, 1)

            for half in range(2):
                for t in range(4 * half, 4 * half + 4):
                    act.wait_ge(s_os, 32 + 24 + t + 1)
                    if t:
                        act.wait_ge(s_x2ss, t)
                    row_squares(x2, t, stat[:, t:t + 1], s_x2ss, junk2)
                act.wait_ge(s_x2ms, half + 1)
                act.activation(stat[:, 8 + 4 * half:12 + 4 * half], stat[:, 4 * half:4 * half + 4],
                               ACT.Sqrt).then_inc(s_x2rt, 1)
            for i in range(2 * KC):
                half, c = i // KC, i % KC
                act.wait_ge(s_x2T, i + 1)
                act.activation(hn_hi[:, c, half * HN:(half + 1) * HN], ps[:, 4 * half + c % 4, :], ACT.Copy,
                               scale=vec[:, V_N2 + c:V_N2 + c + 1]).then_inc(s_hnhi, 1)

            def hidden(g, par, first):
                for s in range(2):
                    act.wait_ge(s_up, 2 * g + s + 1)
                    if not first:
                        act.wait_ge(s_rsq, 2 * g + s - 1)
                    act.activation(relu_t[s][:, :], bank(2 * s, 2), ACT.Relu).then_inc(s_relu, 1)
                    if not (isinstance(g, int) and g < 2):
                        act.wait_ge(s_dn, 16 * g - 16)
                    act.wait_ge(s_rsq, 2 * g + s + 1)
                    act.activation(a_hi[par][:, s, :], relu_sq[s][:, :], ACT.Copy).then_inc(s_ahi, 1)

            hidden(0, 0, True)
            hidden(1, 1, False)
            with act.Fori(1, NFG // 2) as i:
                for par in range(2):
                    hidden(2 * i + par, par, False)

        @block.vector
        def _(dve):
            mine = Count(dve, s_dve)

            def step(instruction):
                mine.add(instruction)
                mine.wait()

            dve.wait_ge(s_tab, 1)
            dve.tensor_copy(vec[:, :], ps[:, 7, 0:N_VEC]).then_inc(s_tabr, 1)
            dve.tensor_copy(cw[:, :, :], ps[:, 6, 0:256].rearrange("p (c j) -> p c j", c=KC)).then_inc(s_tabr, 1)
            step(dve.tensor_scalar(stat[:, 32:48], sink[:, :], -1.0, None, ALU.mult))

            def row_norm(src, dst, half, summed, ms, root, done):
                a, b = 4 * half, 4 * half + 4
                dve.wait_ge(summed, b)
                dve.tensor_scalar(stat[:, a:b], stat[:, a:b], 1.0 / D, EPS, ALU.mult, ALU.add).then_inc(ms, 1)
                dve.wait_ge(root, half + 1)
                step(dve.reciprocal(stat[:, 8 + a:8 + b], stat[:, 8 + a:8 + b]))
                for t in range(a, b):
                    dve.tensor_scalar(dst[:, t, :], src[:, t, :], stat[:, 8 + t:9 + t], None, ALU.mult).then_inc(done, 1)

            def lo_part(i, dst, scale, hi, hi_sem, done):
                half, c = i // KC, i % KC
                cols = slice(half * HN, (half + 1) * HN)
                dve.wait_ge(hi_sem, i + 1)
                dve.scalar_tensor_tensor(out=dst[:, c, cols], in0=ps[:, 4 * half + c % 4, :], scalar=vec[:, scale + c:scale + c + 1],
                                         in1=hi[:, c, cols].bitcast(F32), op0=ALU.mult, op1=ALU.subtract).then_inc(done, 1)

            for half in range(2):
                row_norm(x_tok, x_tok, half, s_xss, s_xms, s_xrt, s_xn)
            for i in range(KC):
                lo_part(i, h_lo, V_N1, h_hi, s_hhi, s_h)

            def qkv_sum(j):
                g, kp, t = j // 32, j // 8 % 4, j % 8
                dst, src = kv_tok[:, t, :], ps[:, j % 4, :]
                if g < 2:
                    dst = q_tok[:, t, g * HN:(g + 1) * HN].rearrange("x (j s d) -> x s j d", j=GRP, s=2)
                    src = src.rearrange("x (s j d) -> x s j d", j=GRP, s=2)
                dve.wait_ge(s_qkvp, j + 1)
                if kp == 0:
                    dve.tensor_copy(dst, src).then_inc(s_qkvs, 1)
                else:
                    dve.wait_ge(s_qkvs, j - 7)
                    dve.tensor_tensor(dst, src, dst, ALU.add).then_inc(s_qkvs, 1)

            def head_steps(i, tok, c0, heads, gain):
                v = tok[:, :, c0:c0 + heads * HD].rearrange("p t (h d) -> p t h d", d=HD)
                rs = head_rs[:, :, 0:heads]

                def sums():
                    for th in range(2):
                        dve.wait_ge(s_sq, 2 * i + th + 1)
                        sq = squares[:, :, 0:heads * HD].rearrange("p t (h d) -> p t h d", d=HD)
                        ins = dve.tensor_reduce(head_ss[:, 4 * th:4 * th + 4, 0:heads], sq, AX.X, ALU.add)
                        ins.then_inc(s_ss, 1)
                    dve.wait_ge(s_ss, 2 * i + 2)
                    dve.tensor_scalar(head_ss[:, :, 0:heads], head_ss[:, :, 0:heads], 1.0 / HD, EPS,
                                      ALU.mult, ALU.add).then_inc(s_ms, 1)

                def norm():
                    dve.wait_ge(s_rt, i + 1)
                    step(dve.reciprocal(rs, rs))
                    for t in range(TT):
                        ins = dve.tensor_tensor(v[:, t], v[:, t], rs[:, t].unsqueeze(2).broadcast_to([P, heads, HD]), ALU.mult)
                    step(ins)

                def gains():
                    for t in range(TT):
                        ins = dve.tensor_tensor(v[:, t], v[:, t], gain[:, :].unsqueeze(1).broadcast_to([P, heads, HD]), ALU.mult)
                    step(ins)

                def rotate():
                    t1, t2 = v[:, :, :, 0:HALF], v[:, :, :, HALF:ROT]
                    cos, sin = (a[:, :, :].unsqueeze(2).broadcast_to([P, TT, heads, HALF]) for a in (cos_sb, sin_sb))
                    r = [x[:, :, 0:heads, :] for x in rope_tmp]
                    dve.tensor_tensor(r[0], t1, cos, ALU.mult)
                    dve.tensor_tensor(r[1], t2, sin, ALU.mult)
                    dve.tensor_tensor(r[2], t2, cos, ALU.mult)
                    step(dve.tensor_tensor(r[3], t1, sin, ALU.mult))
                    dve.tensor_tensor(t1, r[0], r[1], ALU.subtract)
                    dve.tensor_tensor(t2, r[2], r[3], ALU.add).then_inc(s_qk, 1)

                return [sums, norm, gains, rotate]

            q_steps = [head_steps(g, q_tok, g * HN, 8, gq) for g in range(2)]
            k_steps = head_steps(2, kv_tok, 0, N_KV, gk)
            for g in range(3):
                pieces = [[], q_steps[0], q_steps[1]][g]
                for kp in range(4):
                    for t in range(TT):
                        if g == 0 and kp == 0 and t == 4:
                            for i in range(KC, 2 * KC):
                                lo_part(i, h_lo, V_N1, h_hi, s_hhi, s_h)
                        qkv_sum(32 * g + 8 * kp + t)
                    if pieces:
                        pieces[kp]()
            for piece in k_steps:
                piece()
            dve.wait_ge(s_vhi, 1)
            dve.tensor_tensor(v_lo[:, :, :], kv_tok[:, :, KV_W:2 * KV_W], v_hi[:, :, :].bitcast(F32),
                              ALU.subtract).then_inc(s_v, 1)

            def make_glu(c, b):
                dve.wait_ge(s_ca, c + 1)
                dve.wait_ge(s_cs, c + 1)
                g = glu_of(c)[:, PAD:PAD + S]
                dve.tensor_tensor(g, bank(b, 2), g, ALU.mult).then_inc(s_glu, 1)

            def conv_steps(c, first, last):
                g, y_c = glu_of(c), y_of(c)
                for o in range(first, min(last, CSTEPS)):
                    j, c0 = o // 2, o % 2 * HN
                    acc, src = y_c[:, c0:c0 + HN], g[:, c0 + j:c0 + j + HN]
                    if o == 0:
                        dve.wait_ge(s_glu, c + 1)
                        if c >= EARLY + 2:
                            dve.wait_ge(s_sp[c - 2], 16)
                    if j == 0:
                        ins = dve.tensor_scalar(acc, src, cw[:, c, 0:1], vec[:, V_CB + c:V_CB + c + 1], ALU.mult, ALU.add)
                    else:
                        dve.wait_ge(s_cv, CSTEPS * c + o - 1)
                        ins = dve.scalar_tensor_tensor(out=acc, in0=src, scalar=cw[:, c, j:j + 1], in1=acc,
                                                       op0=ALU.mult, op1=ALU.add)
                    ins.then_inc(s_cv, 1)

            for g in glu_early:
                ins = dve.memset(g[:, 0:PAD], 0.0)
            step(ins)
            make_glu(0, 4)

            def mask_scores(G):
                b, kv, i = G // N_KV, G % N_KV, G % 2
                lo = P if b == 0 else 0
                dve.wait_ge(s_sc, G + 1)
                if G >= 2:
                    dve.wait_ge(s_pT, G - 1)
                for j in range(GRP):
                    c0 = (j % 2) * 256
                    ins = dve.tensor_tensor_reduce(probs[i][:, j, lo:], ps[:, 4 + j // 2, c0 + lo:c0 + 256], mask[:, lo:],
                                                   HD ** -0.5, NEG, ALU.add, ALU.max, stat[:, 24 + 4 * i + j:25 + 4 * i + j])
                step(ins)
                neg = stat[:, 4 * i:4 * i + 4]
                sinks_neg = stat[:, 32 + GRP * kv:36 + GRP * kv]
                step(dve.scalar_tensor_tensor(out=neg, in0=stat[:, 24 + 4 * i:28 + 4 * i], scalar=-1.0, in1=sinks_neg,
                                              op0=ALU.mult, op1=ALU.min))
                dve.tensor_tensor(stat[:, 16 + 4 * i:20 + 4 * i], neg, sinks_neg, ALU.subtract).then_inc(s_mx, 1)

            def invert_totals(G):
                i = G % 2
                total = stat[:, 8 + 4 * i:12 + 4 * i]
                dve.wait_ge(s_exp, G + 1)
                step(dve.tensor_tensor(total, total, stat[:, 16 + 4 * i:20 + 4 * i], ALU.add))
                dve.reciprocal(total, total).then_inc(s_rl, 1)

            def pt_low(G):
                lo = 1 if G < N_KV else 0
                dve.wait_ge(s_pThi, G + 1)
                dve.tensor_tensor(pt_lo[:, lo:, :], ps[:, 6 + lo:8, :], pt_hi[:, lo:, :].bitcast(F32),
                                  ALU.subtract).then_inc(s_pTr, 1)

            NG = TT * N_KV
            for G in range(NG + 1):
                if G == 10 or G == 21:
                    make_glu(1 if G == 10 else 2, 0)
                if G < NG:
                    mask_scores(G)
                    c = next(i for i, (a, b) in enumerate(CONV_SPANS) if a <= G < b)
                    first, end = CONV_SPANS[c]
                    share = -(-CSTEPS // (end - first))
                    at = share * (G - first)
                    conv_steps(c, at, at + share // 2)
                    invert_totals(G)
                    conv_steps(c, at + share // 2, at + share)
                if G >= 1:
                    pt_low(G - 1)

            dve.wait_ge(s_pv, NG)
            step(dve.memset(glu_late[:, 0:PAD], 0.0))
            for t in range(TT):
                dve.wait_ge(s_ohi, t + 1)
                dve.tensor_tensor(o_lo[:, t, :, :], o_raw[:, t, :, :], o_hi[:, t, :, :].bitcast(F32),
                                  ALU.subtract).then_inc(s_o, 1)

            def merge_attention(f):
                dve.wait_ge(s_gas, f + 1)
                dve.wait_ge(s_ya, f + 1)
                dve.tensor_tensor(ga[:, f, :], bank(4 + 2 * (f % 2), 2), ga[:, f, :], ALU.mult).then_inc(s_ma, 1)

            for c in range(EARLY, KC):
                make_glu(c, 2)
                at = MIDDLE.index(("a", c)) + 1
                after = MIDDLE[at:at + 3] if c >= 5 else []
                fs = [f for k, f in after if k == "Y"]
                for i, f in enumerate(fs):
                    conv_steps(c, 20 * i, 20 * i + 20)
                    merge_attention(f)
                conv_steps(c, 20 * len(fs), CSTEPS)

            dve.wait_ge(s_cv, CSTEPS * KC)
            for c in range(KC):
                dve.wait_ge(s_yin[c], 16)
                if c == 1:
                    ins = dve.tensor_tensor(y_sum[:, :], y[:, 0, :], y[:, 1, :], ALU.add)
                if c >= 2:
                    ins = dve.tensor_tensor(y_sum[:, :], y_sum[:, :], y[:, c, :], ALU.add)
                if 1 <= c < KC - 1:
                    step(ins)
            ins.then_inc(s_ysum, 1)
            dve.wait_ge(s_mean, 1)

            def add_squares(c):
                dve.wait_ge(s_ysq, c + 1)
                if c > 1:
                    dve.wait_ge(s_ysu, c - 1)
                dve.tensor_tensor(y_sum[:, :], y_sum[:, :], sq_y[c % 2][:, :], ALU.add).then_inc(s_ysu, 1)

            for c in range(KC):
                dve.tensor_tensor(y[:, c, :], y[:, c, :], bank(0, 2), ALU.subtract).then_inc(s_yc, 1)
                if c >= 3:
                    add_squares(c - 2)
            add_squares(KC - 2)
            add_squares(KC - 1)
            dve.wait_ge(s_vsum, 1)
            dve.tensor_scalar(ln_rs[:, :], bank(2, 2), EPS, None, ALU.add).then_inc(s_var, 1)
            dve.wait_ge(s_std, 1)
            step(dve.reciprocal(ln_rs[:, :], ln_rs[:, :]))

            def scale_row(c):
                dve.scalar_tensor_tensor(out=y[:, c, :], in0=y[:, c, :], scalar=vec[:, V_CG + c:V_CG + c + 1],
                                         in1=ln_rs[:, :], op0=ALU.mult, op1=ALU.mult).then_inc(s_z, 1)

            def c_low(c):
                dve.wait_ge(s_chi, c + 1)
                dve.tensor_tensor(c_lo[:, c, :], y[:, c, :], c_hi[:, c, :].bitcast(F32), ALU.subtract).then_inc(s_clo, 1)

            scale_row(0)
            scale_row(1)
            for c in range(KC):
                dve.wait_ge(s_sw, c + 1)
                dve.scalar_tensor_tensor(out=y[:, c, :], in0=y[:, c, :], scalar=vec[:, V_CNB + c:V_CNB + c + 1],
                                         in1=sig[c % 2][:, :], op0=ALU.add, op1=ALU.mult).then_inc(s_c, 1)
                if c + 2 < KC:
                    scale_row(c + 2)
                if c:
                    c_low(c - 1)
            c_low(KC - 1)

            for f in range(KC):
                dve.wait_ge(s_yb, f + 1)
                dve.tensor_tensor(gb[:, f, :], bank(2 * (f % 2), 2), gb[:, f, :], ALU.mult).then_inc(s_mb, 1)
                dve.wait_ge(s_mb, f + 1)
                if f == 0:
                    dve.wait_ge(s_mal, 16 * KC)
                dve.tensor_tensor(gb[:, f, :], gb[:, f, :], ma[:, f, :], ALU.add).then_inc(s_ms2, 1)
                dve.wait_ge(s_mhi, f + 1)
                dve.tensor_tensor(m_lo[:, f, :], gb[:, f, :], m_hi[:, f, :].bitcast(F32), ALU.subtract).then_inc(s_m, 1)

            for j in range(64):
                g, kp, t = j // 32, j // 8 % 4, j % TT
                dst = x2[:, t, g * HN:(g + 1) * HN]
                dve.wait_ge(s_op, j + 1)
                if kp == 0:
                    dve.tensor_copy(dst, ps[:, t % 4, :]).then_inc(s_os, 1)
                    continue
                if kp == 3:
                    dve.wait_ge(s_xa, TT * g + t + 1)
                else:
                    dve.wait_ge(s_os, j - 7)
                dve.tensor_tensor(dst, ps[:, t % 4, :], dst, ALU.add).then_inc(s_os, 1)
                if kp == 2 and t == TT - 1:
                    if g == 0:
                        dve.wait_ge(s_x2in, 16 * TT)
                    for u in range(TT):
                        dst = x2[:, u, g * HN:(g + 1) * HN]
                        dve.wait_ge(s_os, j - 7 + u + 1)
                        dve.tensor_tensor(dst, dst, xr[:, u, g * HN:(g + 1) * HN], ALU.add).then_inc(s_xa, 1)
            for half in range(2):
                row_norm(x2, xn2, half, s_x2ss, s_x2ms, s_x2rt, s_x2n)
            for i in range(2 * KC):
                lo_part(i, hn_lo, V_N2, hn_hi, s_hnhi, s_hn)

            def hidden(g, par, first):
                for s in range(2):
                    dve.wait_ge(s_relu, 2 * g + s + 1)
                    if not first:
                        dve.wait_ge(s_a, 2 * g + s - 1)
                    dve.tensor_tensor(relu_sq[s][:, :], relu_t[s][:, :], relu_t[s][:, :], ALU.mult).then_inc(s_rsq, 1)
                    dve.wait_ge(s_ahi, 2 * g + s + 1)
                    dve.tensor_tensor(a_lo[par][:, s, :], relu_sq[s][:, :], a_hi[par][:, s, :].bitcast(F32),
                                      ALU.subtract).then_inc(s_a, 1)

            def residual(g):
                for j in range(16):
                    s, t = j // 8, j % 8
                    dst = x2[:, t, s * HN:(s + 1) * HN]
                    dve.wait_ge(s_dn, 16 * g + j + 1)
                    if not (isinstance(g, int) and g == 0):
                        dve.wait_ge(s_ds, 16 * g + j - 15)
                    dve.tensor_tensor(dst, ps[:, 4 + t % 4, :], dst, ALU.add).then_inc(s_ds, 1)

            hidden(0, 0, True)
            hidden(1, 1, False)
            residual(0)
            with dve.Fori(0, (NFG - 2) // 2) as i:
                for par in range(2):
                    g = 2 * i + par + 1
                    hidden(g + 1, par, False)
                    residual(g)
            residual(NFG - 1)


INPUTS = ["x", "norm1_g", "w_in", "gate_b", "q_norm_g", "k_norm_g", "sinks", "w_attn_out", "conv_w", "conv_b",
          "conv_norm_g", "conv_norm_b", "w_conv_out", "w_out", "norm2_g", "w_up", "w_down"]


def kernel(**inputs):
    import concourse.bacc as bacc
    from concourse.bass_utils import run_bass_kernel_spmd

    nc = bacc.Bacc("TRN2", target_bir_lowering=False, num_devices=1)
    arrays, args = {}, []
    cos_t, sin_t = rope_tables()
    named = [(n, np.ascontiguousarray(inputs[n])) for n in INPUTS] + [("cos_t", cos_t), ("sin_t", sin_t)]
    for name, a in named:
        arrays[f"in_{name}"] = a
        args.append(nc.dram_tensor(f"in_{name}", a.shape, mybir.dt.from_np(a.dtype), kind="ExternalInput").ap())
    args.append(nc.dram_tensor("out_x", (1, S, D), F32, kind="ExternalOutput").ap())
    hybrid_block(nc, *args)
    return run_bass_kernel_spmd(nc, [arrays], core_ids=[0]).results[0]["out_x"]
```

```python
from contextlib import ExitStack

import numpy as np

import concourse.bass as bass
from concourse import mybir

F32 = mybir.dt.float32
F32R = mybir.dt.float32r
ALU = mybir.AluOpType
ACT = mybir.ActivationFunctionType
AX = mybir.AxisListType

P = 128
D = 1024
S = 1024
KC = D // P
TT = S // P
HN = 512
N_Q, N_KV, HD = 16, 4, 64
GRP = N_Q // N_KV
ROT = HD // 4
HALF = ROT // 2
THETA = 500000.0
Q_W = N_Q * HD
KV_W = N_KV * HD
TAPS = 31
PAD = TAPS - 1
FF = 4 * D
EPS = 1e-6
COL_A = Q_W + 2 * KV_W
COL_G = COL_A + D
COL_GATE = COL_A + 2 * D
COL_GATE2 = COL_GATE + D
SLOTS = 4
FFG = 256
NFG = FF // FFG
NEG = -1e30

MIDDLE = ([("g", 0), ("a", 0), ("g", 1)] + [("a", 1), ("g", 2), ("a", 2), ("A", 0), ("g", 3)]
          + [("a", 3), ("A", 1), ("A", 2), ("A", 3), ("A", 4), ("g", 4), ("a", 4), ("A", 5), ("A", 6), ("A", 7)]
          + [("g", 5), ("a", 5), ("Y", 0), ("Y", 1), ("g", 6), ("a", 6), ("Y", 2), ("Y", 3), ("Y", 4)]
          + [("g", 7), ("a", 7), ("Y", 5), ("Y", 6), ("Y", 7)] + [("B", f) for f in range(8)])
N_QKV, N_COVER, N_ATT, N_YB, N_OUT, N_MLP = 12, 3, 5, 8, 8, 4 * NFG
T_MID = N_QKV
T_ATT = T_MID + N_COVER
T_YB = T_MID + len(MIDDLE)
T_GB = T_YB - KC
T_OUT = T_YB + N_YB
T_MLP = T_OUT + N_OUT
N_TILES = T_MLP + N_MLP
NG = TT * N_KV


def bank_pair(kind, f):
    i = MIDDLE.index((kind, f))
    if kind == "g" or N_COVER <= i < N_COVER + N_ATT:
        return 0
    if kind == "a":
        return 4 if i < N_COVER else 2
    return 4 + 2 * (sum(k in "AYB" for k, _ in MIDDLE[N_COVER + N_ATT:i]) % 2)


def transposed_bank(i):
    return i if i < KC else 4 + i % 4


CSTEPS = 2 * TAPS
SHARE = 5
CONV_FROM = [0, 13, 26]
EARLY = len(CONV_FROM)


def quarters_done(G):
    if G < NG:
        return (G + 1) * (4 * N_ATT - 3) // NG
    return 4 * N_ATT - 3 + (G - NG + 1)


def group_after(tile):
    return 1 + next(G for G in range(NG + 3) if quarters_done(G) >= 4 * tile + 4)


V_N1, V_GA, V_GB, V_CB, V_CG, V_CNB, V_N2 = 0, 8, 16, 24, 32, 40, 48
N_VEC = 56


def rope_tables():
    power = np.power(np.float32(THETA), np.arange(0, ROT, 2, dtype=np.float32) / np.float32(ROT))
    angle = np.arange(S, dtype=np.float32)[:, None] * (np.float32(1.0) / power.astype(np.float32))[None, :]
    return np.cos(angle).astype(np.float32), np.sin(angle).astype(np.float32)


def hybrid_block(nc, x, norm1_g, w_in, gate_b, q_norm_g, k_norm_g, sinks, w_attn_out, conv_w, conv_b,
                 conv_norm_g, conv_norm_b, w_conv_out, w_out, norm2_g, w_up, w_down, cos_t, sin_t, out):
    x_tiles = x[0].rearrange("(t p) d -> t p d", p=P)
    out_tiles = out[0].rearrange("(t p) d -> t p d", p=P)
    base = 16896
    KB = 1024

    with ExitStack() as ctx:
        def sb(name, kb, shape, dt=F32):
            return nc.alloc_sbuf_tensor_at(name, shape, dt, offset=base + int(kb * KB))

        def sem(name):
            return ctx.enter_context(nc.semaphore(name))

        h_hi = sb("h_hi", 0, [P, KC, S], F32R)
        h_lo = sb("h_lo", 32, [P, KC, S], F32R)
        ma = sb("ma", 0, [P, KC, S])
        m_hi = sb("m_hi", 32, [P, KC, S], F32R)
        hn_hi = sb("hn_hi", 0, [P, KC, S], F32R)
        hn_lo = sb("hn_lo", 32, [P, KC, S], F32R)
        x_tok = sb("x_tok", 64, [P, TT, D])
        q_tok = sb("q_tok", 64, [P, TT, Q_W])
        o_raw = sb("o_raw", 64, [P, TT, KC, P])
        o_lo = sb("o_lo", 64, [P, TT, KC, P], F32R)
        y = sb("y", 64, [P, KC, S])
        c_lo = sb("c_lo", 64, [P, KC, S], F32R)
        x2 = sb("x2", 64, [P, TT, D])
        kv_tok = sb("kv_tok", 96, [P, TT, 2 * KV_W])
        cos_sb = sb("cos_sb", 112, [P, TT, HALF])
        sin_sb = sb("sin_sb", 112.25, [P, TT, HALF])
        gq = sb("gq", 112.5, [P, HD])
        gk = sb("gk", 112.75, [P, HD])
        ga = sb("ga", 96, [P, KC, S])
        c_hi = sb("c_hi", 96, [P, KC, S], F32R)
        xr = sb("xr", 96, [P, TT, D])
        GLU_W = PAD + S
        y_early = [sb(f"y_early{c}", at, [P, S]) for c, at in enumerate((100, 104, 119.75))]
        glu_early = [sb(f"glu_early{c}", at, [P, GLU_W]) for c, at in enumerate((113, 108, 123.875))]
        a_hi = [sb(f"a_hi{i}", 96 + 16 * i, [P, 2, S], F32R) for i in range(2)]
        a_lo = [sb(f"a_lo{i}", 104 + 16 * i, [P, 2, S], F32R) for i in range(2)]
        w_hi = [sb(f"w_hi{i}", 128 + 8 * i, [P, D], F32R) for i in range(SLOTS)]
        w_raw = [sb(f"w_raw{i}", 132 + 8 * i, [P, D]) for i in range(SLOTS)]
        w_lo = [sb(f"w_lo{i}", 132 + 8 * i, [P, D], F32R) for i in range(SLOTS)]
        junk = sb("junk", 160, [P, D])
        cw_rows = sb("cw_rows", 164, [32, D])
        vec_rows = sb("vec_rows", 168, [N_VEC, P])
        k_t = sb("k_t", 160, [P, 2, S])
        v_sb = sb("v_sb", 168, [P, TT, KV_W])
        squares = sb("squares", 184, [P, 4, HN])
        rope_tmp = [sb(f"rope_tmp{i}", 192 + 2 * i, [P, TT, 8, HALF]) for i in range(4)]
        head_ss = sb("head_ss", 200, [P, TT, 8])
        head_rs = sb("head_rs", 200.25, [P, TT, 8])
        probs = [sb(f"probs{i}", 176 + 4 * i, [P, GRP, 2 * P]) for i in range(3)]
        minus_top, total, sink_term, top = (sb(n, 188 + i / 8, [P, 3, GRP]) for i, n in
                                            enumerate(("minus_top", "total", "sink_term", "top")))
        pt = [sb(f"pt{i}", 192 + 4 * i, [P, 2, HN]) for i in range(2)]
        q_t = [sb(f"q_t{i}", 200 + 2 * i, [P, HN]) for i in range(2)]
        mask = sb("mask", 204, [P, 2 * P])
        o_hi = sb("o_hi", 160, [P, TT, KC, P], F32R)
        gb = sb("gb", 160, [P, KC, S])
        m_lo = sb("m_lo", 160, [P, KC, S], F32R)
        glu_late = sb("glu_late", 192, [P, GLU_W])
        y_late = [sb(f"y_late{i}", 196.25 + 4 * i, [P, S]) for i in range(2)]
        y_sum = sb("y_sum", 192, [P, S])
        ln_rs = sb("ln_rs", 192, [P, S])
        sq_y = [sb(f"sq_y{i}", 196 + 4 * i, [P, S]) for i in range(2)]
        sig = [sb(f"sig{i}", 196 + 4 * i, [P, S]) for i in range(2)]
        junk2 = sb("junk2", 192, [P, D])
        diag = sb("diag", 196, [P, TT, P])
        relu_t = [sb(f"relu_t{i}", 160 + 4 * i, [P, S]) for i in range(2)]
        relu_sq = [sb(f"relu_sq{i}", 168 + 4 * i, [P, S]) for i in range(2)]
        small = 205 * KB
        ident = sb("ident", small / KB, [P, P])
        mean_w = sb("mean_w", (small + 512) / KB, [P, P])
        vec = sb("vec", (small + 1024) / KB, [P, N_VEC])
        cw = sb("cw", (small + 1248) / KB, [P, KC, 32])
        sink = sb("sink", (small + 2272) / KB, [P, N_Q])
        stat = sb("stat", (small + 2336) / KB, [P, 24])
        sinks_neg = sb("sinks_neg", (small + 2432) / KB, [P, N_Q])

        y_dram = nc.dram_tensor("y_spilled", (KC, P, S), F32).ap()
        ma_dram = nc.dram_tensor("ma_spilled", (KC, P, S), F32).ap()

        def glu_of(c):
            return glu_early[c] if c < EARLY else glu_late

        def y_of(c):
            return y_early[c] if c < EARLY else y_late[c % 2]

        ps = ctx.enter_context(nc.psum_tensor("ps", [P, 8, HN], F32))

        def bank(b, n=1):
            return ps[:, b:b + n, :].rearrange("p b n -> p (b n)")

        s_x = [sem(f"x_landed{t}") for t in range(TT)]
        s_vecs = sem("channel_vectors_landed")
        s_cwin = sem("conv_taps_landed")
        s_small = sem("small_inputs_landed")
        s_cwzero = sem("conv_taps_zeroed")
        s_ident = sem("identity_built")
        s_landed = [sem(f"weights_landed{i}") for i in range(SLOTS)]
        s_seen = sem("weights_seen")
        s_hi = sem("weights_hi_split")
        s_split = sem("weights_split")
        s_begun = sem("tiles_begun")
        s_dve = sem("vector_steps")
        s_tab = sem("tables_transposed")
        s_tabr = sem("tables_ready")
        s_warm = sem("root_table_loaded")
        s_xss = sem("x_squares_summed")
        s_xms = sem("x_mean_square")
        s_xrt = sem("x_root")
        s_xd = sem("x_diagonals")
        s_xT = sem("x_transposed")
        s_hhi = sem("h_hi_ready")
        s_h = sem("h_ready")
        s_qkvp = sem("qkv_partial")
        s_qkvs = sem("qkv_summed")
        s_sq = sem("head_squares")
        s_ss = sem("head_squares_summed")
        s_ms = sem("head_mean_square")
        s_rt = sem("head_root")
        s_qk = sem("heads_ready")
        s_v = sem("v_ready")
        s_kT = sem("k_transposed")
        s_kTr = sem("k_t_ready")
        s_qT = sem("q_transposed")
        s_qTr = sem("q_t_ready")
        s_sc = sem("scores")
        s_mx = sem("scores_masked")
        s_exp = sem("exps")
        s_rl = sem("totals_inverted")
        s_pn = sem("probs_normalised")
        s_pT = sem("probs_transposed")
        s_pTr = sem("pt_ready")
        s_pv = sem("values_mixed")
        s_oe = sem("o_stored")
        s_ga = sem("gate_a_logits")
        s_gas = sem("gate_a_ready")
        s_ohi = sem("o_hi_ready")
        s_o = sem("o_ready")
        s_ya = sem("y_attn")
        s_ma = sem("attn_merged")
        s_ca = sem("conv_a")
        s_cg = sem("conv_gate")
        s_cs = sem("conv_sigmoid")
        s_glu = sem("glu_ready")
        s_cv = sem("conv_steps")
        s_sp = [sem(f"y_spilled{c}") for c in range(KC)]
        s_masp = sem("attn_merged_spilled")
        s_mal = sem("attn_merged_reloaded")
        s_yin = [sem(f"y_reloaded{c}") for c in range(KC)]
        s_ysum = sem("y_summed")
        s_gbl = sem("gate_b_logits")
        s_gb = sem("gate_b_ready")
        s_mean = sem("mean_ready")
        s_yc = sem("centred")
        s_ysq = sem("centred_squares")
        s_ysu = sem("squares_added")
        s_vsum = sem("variance_summed")
        s_var = sem("variance_ready")
        s_std = sem("std_ready")
        s_z = sem("ln_scaled")
        s_sw = sem("ln_sigmoid")
        s_c = sem("conv_out_ready")
        s_chi = sem("c_hi_ready")
        s_clo = sem("c_ready")
        s_yb = sem("y_conv")
        s_mb = sem("y_conv_read")
        s_ms2 = sem("merged")
        s_mhi = sem("m_hi_ready")
        s_m = sem("m_ready")
        s_x2in = sem("x_reloaded")
        s_xa = sem("residual_added")
        s_op = sem("out_partial")
        s_os = sem("out_summed")
        s_x2ss = sem("x2_squares_summed")
        s_x2ms = sem("x2_mean_square")
        s_x2rt = sem("x2_root")
        s_x2d = sem("x2_diagonals")
        s_x2T = sem("x2_transposed")
        s_hnhi = sem("hn_hi_ready")
        s_hn = sem("hn_ready")
        s_up = sem("up_done")
        s_relu = sem("relu_done")
        s_rsq = sem("relu_squared")
        s_ahi = sem("a_hi_ready")
        s_a = sem("a_ready")
        s_dn = sem("down_partial")
        s_ds = sem("down_summed")
        s_out = sem("output_stored")

        block = ctx.enter_context(nc.Block())

        def column_tile(w, c0):
            return w.rearrange("(k p) n -> p k n", p=P)[:, :, bass.ds(c0, P)]

        def row_tile(w, k0, c0):
            return w[bass.ds(k0, 2 * P), bass.ds(c0, HN)].rearrange("(k p) n -> p k n", p=P)

        @block.sync
        def _(sp):
            def load(n, slot, src, wait=True):
                if wait:
                    sp.wait_ge(s_begun, n - SLOTS + 2)
                k = src.shape[1]
                sp.dma_start(w_raw[slot][:, :].rearrange("p (k n) -> p k n", k=k), src).then_inc(s_landed[slot], 16)

            for t in range(TT):
                if t == TT // 2:
                    for r, v in ((V_N1, norm1_g[0]), (V_GA, gate_b[0]), (V_CB, conv_b[0]),
                                 (V_CG, conv_norm_g[0]), (V_CNB, conv_norm_b[0]), (V_N2, norm2_g[0])):
                        n = v.shape[0] // P
                        sp.dma_start(vec_rows[r:r + n, :], v.rearrange("(r c) -> r c", c=P)).then_inc(s_vecs, 16)
                    load(0, 0, row_tile(w_in[0], 0, 0), wait=False)
                sp.dma_start(x_tok[:, t, :], x_tiles[t]).then_inc(s_x[t], 16)
            sp.dma_start(gq[:, :], q_norm_g.partition_broadcast(P)).then_inc(s_small, 16)
            sp.dma_start(gk[:, :], k_norm_g.partition_broadcast(P)).then_inc(s_small, 16)
            sp.dma_start(sink[:, :], sinks.partition_broadcast(P)).then_inc(s_small, 16)
            sp.dma_start(cos_sb[:, :, :], cos_t.rearrange("(t p) h -> p t h", p=P)).then_inc(s_small, 16)
            sp.dma_start(sin_sb[:, :, :], sin_t.rearrange("(t p) h -> p t h", p=P)).then_inc(s_small, 16)
            for g, c0 in enumerate((0, HN, Q_W)):
                for kp in range(0 if g else 1, 4):
                    load(4 * g + kp, kp, row_tile(w_in[0], 2 * P * kp, c0), wait=g > 0)
            for i, (kind, f) in enumerate(MIDDLE):
                n = T_MID + i
                if n == T_GB + 3 or n == T_GB + 4:
                    sp.wait_ge(s_begun, T_GB + 1)
                    for c in range(KC - 1) if n == T_GB + 3 else [KC - 1]:
                        sp.wait_ge(s_sp[c], 16)
                        sp.dma_start(y[:, c, :], y_dram[c]).then_inc(s_yin[c], 16)
                w, c0 = {"g": (w_in, COL_G), "a": (w_in, COL_A), "A": (w_in, COL_GATE), "B": (w_in, COL_GATE2),
                         "Y": (w_attn_out, 0)}[kind]
                load(n, n % SLOTS, column_tile(w[0], c0 + f * P))
            for f in range(N_YB):
                n = T_YB + f
                if f == 3:
                    sp.wait_ge(s_begun, T_YB + 1)
                    sp.wait_ge(s_masp, 16 * KC)
                    for c in range(KC):
                        sp.dma_start(ma[:, c, :], ma_dram[c]).then_inc(s_mal, 16)
                load(n, n % SLOTS, column_tile(w_conv_out[0], f * P))
            for j in range(N_OUT):
                n = T_OUT + j
                if j == 3:
                    sp.wait_ge(s_begun, T_OUT + 1)
                    for t in range(TT):
                        sp.dma_start(xr[:, t, :], x_tiles[t]).then_inc(s_x2in, 16)
                load(n, n % SLOTS, row_tile(w_out[0], 2 * P * (j % 4), (j // 4) * HN))

            for s in range(2):
                load(T_MLP + s, s, column_tile(w_up[0], s * P))
            with sp.Fori(0, NFG - 1) as g:
                for s in range(2):
                    load(T_MLP + 2 + 4 * g + s, 2 + s, column_tile(w_up[0], (2 * g + 2 + s) * P))
                for s in range(2):
                    load(T_MLP + 4 + 4 * g + s, s, row_tile(w_down[0], g * FFG, s * HN))
            for s in range(2):
                load(N_TILES - 2 + s, 2 + s, row_tile(w_down[0], FF - FFG, s * HN))
            for t in range(TT):
                sp.wait_ge(s_ds, 16 * (NFG - 1) + 8 + t + 1)
                sp.dma_start(out_tiles[t], x2[:, t, :]).then_inc(s_out, 16)
            sp.wait_ge(s_out, 16 * TT)

        @block.gpsimd
        def _(pool):
            pool.memset(cw_rows[:, :], 0.0).then_inc(s_cwzero, 1)
            pool.memset(ident[:, :], 0.0).then_inc(s_ident, 1)
            pool.memset(mean_w[:, :], 1.0 / D).then_inc(s_ident, 1)
            pool.memset(mask[:, :], 0.0).then_inc(s_ident, 1)
            pool.wait_ge(s_ident, 3)
            pool.affine_select(out=ident[:, :], in_=ident[:, :], compare_op=ALU.not_equal, fill=1.0,
                               base=0, pattern=[[-1, P]], channel_multiplier=1).then_inc(s_ident, 1)
            pool.affine_select(out=mask[:, 0:P], in_=mask[:, 0:P], compare_op=ALU.is_gt, fill=NEG,
                               base=0, pattern=[[1, P]], channel_multiplier=-1).then_inc(s_ident, 1)
            pool.affine_select(out=mask[:, P:2 * P], in_=mask[:, P:2 * P], compare_op=ALU.is_ge, fill=NEG,
                               base=0, pattern=[[-1, P]], channel_multiplier=1).then_inc(s_ident, 1)
            def split(i, s):
                pool.wait_ge(s_landed[s], 16 * i + 16)
                pool.sem_inc(s_seen, 1)
                pool.tensor_copy(w_hi[s][:, :], w_raw[s][:, :]).then_inc(s_hi, 1)
                pool.wait_ge(s_hi, SLOTS * i + s + 1)
                pool.tensor_tensor(w_lo[s][:, :], w_raw[s][:, :], w_hi[s][:, :].bitcast(F32),
                                   ALU.subtract).then_inc(s_split, 1)

            with pool.Fori(0, N_TILES // SLOTS) as i:
                for s in range(SLOTS):
                    split(i, s)

        @block.tensor
        def _(pe):
            def column_product(n, slot, b, rhs_hi, rhs_lo, ks=range(KC), chunk_ready=None):
                pe.wait_ge(s_split, n + 1)
                wh = w_hi[slot][:, :].rearrange("p (k m) -> p k m", k=KC)
                wl = w_lo[slot][:, :].rearrange("p (k m) -> p k m", k=KC)
                for k in ks:
                    first, last = k == 0, k == KC - 1
                    if chunk_ready:
                        pe.wait_ge(*chunk_ready(k))
                    for h in range(2):
                        o = ps[:, b + h, :]
                        mm = pe.matmul(o, wh[:, k, :], rhs_hi(k, h), start=first, stop=False)
                        if first and h == 0:
                            mm.then_inc(s_begun, 1)
                        pe.matmul(o, wh[:, k, :], rhs_lo(k, h), start=False, stop=False)
                    for h in range(2):
                        o = ps[:, b + h, :]
                        mm = pe.matmul(o, wl[:, k, :], rhs_hi(k, h), start=False, stop=last)
                return mm

            def row_product(b, lhs_hi, lhs_lo, slot, begins):
                wh = w_hi[slot][:, :].rearrange("p (k n) -> p k n", k=2)
                wl = w_lo[slot][:, :].rearrange("p (k n) -> p k n", k=2)
                for k in range(2):
                    mm = pe.matmul(ps[:, b, :], lhs_hi(k), wh[:, k, :], start=k == 0, stop=False)
                    if begins and k == 0:
                        mm.then_inc(s_begun, 1)
                    pe.matmul(ps[:, b, :], lhs_hi(k), wl[:, k, :], start=False, stop=False)
                    mm = pe.matmul(ps[:, b, :], lhs_lo(k), wh[:, k, :], start=False, stop=k == 1)
                return mm

            def halves(a):
                return lambda k, h: a[:, k, h * HN:(h + 1) * HN]

            pe.wait_ge(s_ident, 4)
            pe.wait_ge(s_vecs, 16 * 6)
            pe.wait_ge(s_cwin, 16)
            pe.transpose(ps[:, 7, 0:N_VEC], vec_rows[:, :], ident[0:N_VEC, 0:N_VEC])
            for c in range(KC):
                mm = pe.transpose(ps[:, 6, 32 * c:32 * c + 32], cw_rows[:, c * P:(c + 1) * P], ident[0:32, 0:32])
            mm.then_inc(s_tab, 1)

            def transposed(src, half, c, i, free, done, ready):
                b = transposed_bank(i)
                if half:
                    pe.wait_ge(free, i - 3)
                elif c == 6:
                    pe.wait_ge(s_tabr, 2)
                if c == 0:
                    pe.wait_ge(ready, 4 * half + 4)
                for j in range(4):
                    mm = pe.matmul(ps[:, b, j * P:(j + 1) * P], src[:, 4 * half + j, c * P:(c + 1) * P],
                                   diag[:, 4 * half + j, :], start=True, stop=True)
                mm.then_inc(done, 1)

            def h_transposes(half):
                for c in range(KC):
                    transposed(x_tok, half, c, half * KC + c, s_h, s_xT, s_xd)

            h_transposes(0)
            j = 0
            for g in range(3):
                for kp in range(4):
                    pe.wait_ge(s_split, 4 * g + kp + 1)
                    for t in range(TT):
                        if j < 4:
                            pe.wait_ge(s_h, max(j + 1, 2))
                        if j == 4:
                            h_transposes(1)
                            pe.wait_ge(s_h, 2 * KC)
                        if j >= 8:
                            pe.wait_ge(s_qkvs, j - 7)
                        mm = row_product(t, lambda k: h_hi[:, 2 * kp + k, t * P:(t + 1) * P],
                                         lambda k: h_lo[:, 2 * kp + k, t * P:(t + 1) * P], kp, t == 0)
                        mm.then_inc(s_qkvp, 1)
                        j += 1

            read_by = {"g": s_cs, "a": s_glu, "A": s_gas, "Y": s_ma, "B": s_gb}
            signals = {"g": s_cg, "a": s_ca, "A": s_ga, "Y": s_ya, "B": s_gbl}

            def middle_tile(i, part=None):
                kind, f = MIDDLE[i]
                rhs = (o_rhs(o_hi), o_rhs(o_lo)) if kind == "Y" else (halves(h_hi), halves(h_lo))
                b = bank_pair(kind, f)
                before = [e for e in range(i) if bank_pair(*MIDDLE[e]) == b]
                if part in (None, 0) and before:
                    k, e = MIDDLE[before[-1]]
                    pe.wait_ge(read_by[k], e + 1)
                ks = range(KC) if part is None else range(2 * part, 2 * part + 2)
                mm = column_product(T_MID + i, (T_MID + i) % SLOTS, b, *rhs, ks)
                if part in (None, 3):
                    mm.then_inc(signals[kind], 1)

            o_rhs = lambda o: (lambda k, h: o[:, 4 * h:4 * h + 4, k, :])

            def q_unit(u):
                b, p = u // 2, u % 2
                if u >= 1:
                    pe.wait_ge(s_qTr, u)
                for j in range(GRP):
                    c0 = (p * GRP + j) * P
                    mm = pe.transpose(ps[:, 3, j * P:(j + 1) * P], q_tok[:, b, c0:c0 + P], ident[:, :])
                mm.then_inc(s_qT, 1)

            def scores(G):
                b, kv = G // N_KV, G % N_KV
                p, s = kv // 2, kv % 2
                r = slice(64 * s, 64 * s + 64)
                pe.wait_ge(s_qTr, G // 2 + 1)
                if G:
                    pe.wait_ge(s_mx, G)
                else:
                    pe.wait_ge(s_glu, 1)
                keys = slice(max(b - 1, 0) * P, (b + 1) * P)
                lo = P if b == 0 else 0
                for j in range(GRP):
                    c0 = (j % 2) * 256
                    mm = pe.matmul(ps[:, 4 + j // 2, c0 + lo:c0 + 256], q_t[(G // 2) % 2][r, j * P:(j + 1) * P],
                                   k_t[r, p, keys], start=True, stop=True)
                mm.then_inc(s_sc, 1)

            def turn_probs(G):
                pe.wait_ge(s_pn, G + 1)
                if G:
                    pe.wait_ge(s_pTr, G)
                for hf in range(1 if G < N_KV else 0, 2):
                    for j in range(GRP):
                        mm = pe.transpose(ps[:, 6 + hf, j * P:(j + 1) * P],
                                          probs[G % 3][:, j, hf * P:(hf + 1) * P], ident[:, :])
                mm.then_inc(s_pT, 1)

            def mix_values(G):
                b, kv = G // N_KV, G % N_KV
                pe.wait_ge(s_pTr, G + 1)
                if G:
                    pe.wait_ge(s_oe, G)
                else:
                    pe.wait_ge(s_v, 1)
                hs = [1] if b == 0 else [0, 1]
                for hf in hs:
                    mm = pe.matmul(ps[:, 2, :], v_sb[:, b - 1 + hf, kv // 2 * P:(kv // 2 + 1) * P], pt[G % 2][:, hf, :],
                                   start=hf == hs[0], stop=hf == 1)
                mm.then_inc(s_pv, 1)

            pe.wait_ge(s_qkvs, 88 + 2)
            middle_tile(0)
            pe.wait_ge(s_qkvs, 88 + 6)
            middle_tile(1)
            pe.wait_ge(s_qk, 3)
            for i, b in enumerate((6, 7, 2, 3)):
                for t in range(4):
                    mm = pe.transpose(ps[:, b, t * P:(t + 1) * P],
                                      kv_tok[:, 4 * (i % 2) + t, i // 2 * P:(i // 2 + 1) * P], ident[:, :])
                mm.then_inc(s_kT, 1)
            middle_tile(2, 0)
            middle_tile(2, 1)
            pe.wait_ge(s_kTr, 4)
            q_unit(0)
            middle_tile(2, 2)
            q_unit(1)
            scores(0)
            middle_tile(2, 3)
            for G in range(NG + 3):
                if G < NG:
                    if G:
                        scores(G)
                    if G % 4 == 2 and G + 2 < NG:
                        q_unit((G + 2) // 2)
                    if G % 4 == 3 and G + 1 < NG:
                        q_unit((G + 1) // 2 + 1)
                for q in range(quarters_done(G - 1) if G else 0, quarters_done(G)):
                    middle_tile(N_COVER + q // 4, q % 4)
                if G >= 3:
                    mix_values(G - 3)
                if 2 <= G < NG + 2:
                    turn_probs(G - 2)

            pe.wait_ge(s_mx, NG)
            pe.wait_ge(s_pTr, NG)
            pe.wait_ge(s_oe, NG)
            for i in range(N_COVER + N_ATT, len(MIDDLE) - KC):
                if MIDDLE[i] == ("Y", 0):
                    pe.wait_ge(s_o, TT)
                middle_tile(i)

            def channel_sum(b, src, ready, count, done):
                pe.wait_ge(ready, count)
                for h in range(2):
                    mm = pe.matmul(ps[:, b + h, :], mean_w[:, :], src[:, h * HN:(h + 1) * HN], start=True, stop=True)
                mm.then_inc(done, 1)

            for f in range(KC):
                i = len(MIDDLE) - KC + f
                if f == 2:
                    middle_tile(i, 0)
                    channel_sum(0, y_sum, s_ysum, 1, s_mean)
                    for part in range(1, 4):
                        middle_tile(i, part)
                else:
                    middle_tile(i)
                if f == 3:
                    channel_sum(2, y_sum, s_ysu, KC - 1, s_vsum)

            def eight_tiles(first_tile, rhs_hi, rhs_lo, done, free):
                with pe.Fori(0, 2) as i:
                    for s in range(SLOTS):
                        f = SLOTS * i + s
                        if s >= 2:
                            pe.wait_ge(free, f - 1)
                        mm = column_product(first_tile + f, s, 2 * s, rhs_hi, rhs_lo)
                        mm.then_inc(done, 1)
                    pe.wait_ge(free, SLOTS * i + 2)

            pe.wait_ge(s_gb, KC)
            pe.wait_ge(s_clo, KC)
            eight_tiles(T_YB, halves(c_hi), halves(c_lo), s_yb, s_mb)

            for g in range(2):
                for kp in range(SLOTS):
                    if g == 0:
                        pe.wait_ge(s_m, 2 * kp + 2)
                    pe.wait_ge(s_split, T_OUT + SLOTS * g + kp + 1)
                    for t in range(TT):
                        j = 32 * g + kp * TT + t
                        if j >= 8:
                            pe.wait_ge(s_os, j - 7)
                        elif t % 2 == 0:
                            pe.wait_ge(s_mb, KC - 3 + t // 2)
                        mm = row_product(t, lambda k: m_hi[:, 2 * kp + k, t * P:(t + 1) * P],
                                         lambda k: m_lo[:, 2 * kp + k, t * P:(t + 1) * P], kp, t == 0)
                        mm.then_inc(s_op, 1)

            for half in range(2):
                for c in range(KC):
                    if half == 0:
                        pe.wait_ge(s_os, 64 - 8 + c + 1)
                    transposed(x2, half, c, half * KC + c, s_hn, s_x2T, s_x2d)

            def up(g, n, slot0):
                for s in range(2):
                    if not (isinstance(g, int) and g == 0):
                        pe.wait_ge(s_relu, 2 * g + s - 1)
                    ready = (lambda k: (s_hn, KC + k + 1)) if isinstance(g, int) and g == 0 and s == 0 else None
                    mm = column_product(n + s, slot0 + s, 2 * s, halves(hn_hi), halves(hn_lo), chunk_ready=ready)
                    mm.then_inc(s_up, 1)

            def down(g, parity, n, slot0):
                pe.wait_ge(s_a, 2 * g + 2)
                for s in range(2):
                    pe.wait_ge(s_split, n + s + 1)
                    for t in range(TT):
                        if not (isinstance(g, int) and g == 0 and s == 0 and t < 4):
                            pe.wait_ge(s_ds, 16 * g + 8 * s + t - 3)
                        mm = row_product(4 + t % 4, lambda k: a_hi[parity][:, k, t * P:(t + 1) * P],
                                         lambda k: a_lo[parity][:, k, t * P:(t + 1) * P], slot0 + s, t == 0)
                        mm.then_inc(s_dn, 1)

            up(0, T_MLP, 0)
            up(1, T_MLP + 2, 2)
            down(0, 0, T_MLP + 4, 0)
            with pe.Fori(0, (NFG - 2) // 2) as i:
                for par in range(2):
                    g = 2 * i + par + 1
                    up(g + 1, T_MLP + 2 + 4 * g, 2)
                    down(g, (par + 1) % 2, T_MLP + 4 + 4 * g, 0)
            down(NFG - 1, 1, N_TILES - 2, 2)

        @block.scalar
        def _(act):
            act.wait_ge(s_cwzero, 1)
            act.dma_start(cw_rows[0:TAPS, :], conv_w[0]).then_inc(s_cwin, 16)
            act.wait_ge(s_ident, 2)
            act.activation(stat[:, 16:17], mean_w[:, 0:1], ACT.Sqrt).then_inc(s_warm, 1)

            def row_squares(src, t, ss, done, trash=junk):
                act.activation(trash[:, :], src[:, t, :], ACT.Square, accum_out=ss).then_inc(done, 1)

            def x_squares(t):
                act.wait_ge(s_x[t], 16)
                if t:
                    act.wait_ge(s_xss, t)
                row_squares(x_tok, t, stat[:, t:t + 1], s_xss)

            def x_root(half):
                act.wait_ge(s_xms, half + 1)
                act.activation(stat[:, 8 + 4 * half:12 + 4 * half], stat[:, 4 * half:4 * half + 4],
                               ACT.Sqrt).then_inc(s_xrt, 1)

            def h_high(i):
                half, c = i // KC, i % KC
                act.wait_ge(s_xT, i + 1)
                act.activation(h_hi[:, c, half * HN:(half + 1) * HN], ps[:, transposed_bank(i), :], ACT.Copy,
                               scale=vec[:, V_N1 + c:V_N1 + c + 1]).then_inc(s_hhi, 1)

            for t in range(4):
                x_squares(t)
            x_root(0)
            act.wait_ge(s_tabr, 2)
            for t in range(4, TT):
                h_high(2 * (t - 4))
                h_high(2 * (t - 4) + 1)
                x_squares(t)
            x_root(1)
            for i in range(KC, 2 * KC):
                h_high(i)

            def head_squares(tok, c0, heads, summed, i0):
                for th in range(2):
                    act.wait_ge(s_qkvs, summed + 4 * th + 4)
                    if i0 + th:
                        act.wait_ge(s_ss, i0 + th)
                    act.activation(squares[:, :, 0:heads * HD], tok[:, 4 * th:4 * th + 4, c0:c0 + heads * HD],
                                   ACT.Square).then_inc(s_sq, 1)

            def head_root(i, heads):
                act.wait_ge(s_ms, i + 1)
                act.activation(head_rs[:, :, 0:heads], head_ss[:, :, 0:heads], ACT.Sqrt).then_inc(s_rt, 1)

            head_squares(q_tok, 0, 8, 24, 0)
            head_root(0, 8)
            head_squares(q_tok, HN, 8, 32 + 24, 2)
            head_root(1, 8)
            head_squares(kv_tok, 0, N_KV, 64 + 24, 4)
            head_root(2, N_KV)
            act.activation(v_sb[:, :, :], kv_tok[:, :, KV_W:2 * KV_W], ACT.Copy).then_inc(s_v, 1)

            def conv_gate(c):
                act.wait_ge(s_cg, c + 1)
                if c > EARLY:
                    act.wait_ge(s_cv, CSTEPS * c)
                act.activation(glu_of(c)[:, PAD:PAD + S], bank(0, 2), ACT.Sigmoid).then_inc(s_cs, 1)

            def store_gate_a(f):
                act.wait_ge(s_ga, f + 1)
                act.activation(ga[:, f, :], bank(bank_pair("A", f), 2), ACT.Sigmoid, bias=vec[:, V_GA + f:V_GA + f + 1]).then_inc(s_gas, 1)

            def store_gate_b(f):
                act.wait_ge(s_gbl, f + 1)
                act.activation(gb[:, f, :], bank(bank_pair("B", f), 2), ACT.Sigmoid, bias=vec[:, V_GB + f:V_GB + f + 1]).then_inc(s_gb, 1)

            conv_gate(0)
            for i, b in enumerate((6, 7, 2, 3)):
                act.wait_ge(s_kT, i + 1)
                act.activation(k_t[:, i // 2, (i % 2) * HN:(i % 2 + 1) * HN], ps[:, b, :], ACT.Copy).then_inc(s_kTr, 1)

            def q_store(u):
                act.wait_ge(s_qT, u + 1)
                if u >= 2:
                    act.wait_ge(s_sc, 2 * (u - 1))
                act.activation(q_t[u % 2][:, :], ps[:, 3, :], ACT.Copy).then_inc(s_qTr, 1)

            def exps(G):
                i = G % 3
                lo = P if G < N_KV else 0
                act.wait_ge(s_mx, G + 1)
                for j in range(GRP):
                    pr = probs[i][:, j, lo:]
                    act.activation(pr, pr, ACT.Exp, bias=minus_top[:, i, j:j + 1], accum_out=total[:, i, j:j + 1])
                act.activation(sink_term[:, i, :], sink_term[:, i, :], ACT.Exp).then_inc(s_exp, 1)

            def normalise(G):
                i, lo = G % 3, P if G < N_KV else 0
                act.wait_ge(s_rl, G + 1)
                for j in range(GRP):
                    pr = probs[i][:, j, lo:]
                    ins = act.activation(pr, pr, ACT.Copy, scale=total[:, i, j:j + 1])
                ins.then_inc(s_pn, 1)

            def store_o(G):
                b, kv = G // N_KV, G % N_KV
                act.wait_ge(s_pv, G + 1)
                r0 = 64 * (kv % 2)
                for r in range(2):
                    src = ps[r0:r0 + 64, 2, :].rearrange("p (jj s n) -> p jj s n", jj=2, s=2)[:, :, r, :]
                    ins = act.activation(o_raw[64 * r:64 * r + 64, b, 2 * kv:2 * kv + 2, :], src, ACT.Copy)
                ins.then_inc(s_oe, 1)

            def pt_store(G):
                lo = 1 if G < N_KV else 0
                act.wait_ge(s_pT, G + 1)
                if G >= 2:
                    act.wait_ge(s_pv, G - 1)
                act.activation(pt[G % 2][:, lo:, :], ps[:, 6 + lo:8, :], ACT.Copy).then_inc(s_pTr, 1)

            q_store(0)
            q_store(1)
            conv_gate(1)
            for G in range(NG + 3):
                if G == group_after(1):
                    conv_gate(2)
                if G == group_after(3):
                    act.wait_ge(s_v, 1)
                    store_gate_a(0)
                if G < NG:
                    if G % 4 == 2 and G + 2 < NG:
                        q_store((G + 2) // 2)
                    if G % 4 == 3 and G + 1 < NG:
                        q_store((G + 1) // 2 + 1)
                    exps(G)
                if 1 <= G <= NG:
                    normalise(G - 1)
                if G >= 3:
                    store_o(G - 3)
                if 2 <= G < NG + 2:
                    pt_store(G - 2)

            def spill_y(c):
                act.wait_ge(s_cv, CSTEPS * c + CSTEPS)
                act.dma_start(y_dram[c], y_of(c)[:, :]).then_inc(s_sp[c], 16)

            def spill_ma(f):
                act.wait_ge(s_ma, f + 1)
                act.dma_start(ma_dram[f], ga[:, f, :]).then_inc(s_masp, 16)

            act.wait_ge(s_oe, NG)
            for t in range(TT):
                act.activation(o_hi[:, t, :, :], o_raw[:, t, :, :], ACT.Copy).then_inc(s_ohi, 1)
            for c in range(EARLY - 1):
                spill_y(c)
            conv_gate(EARLY)
            for kind, f in MIDDLE[N_COVER + N_ATT:-KC]:
                if kind == "g":
                    if f == EARLY + 1:
                        spill_y(EARLY - 1)
                    spill_y(f - 1)
                    conv_gate(f)
                if kind == "A":
                    if f == 1:
                        act.wait_ge(s_sp[0], 16)
                        act.wait_ge(s_sp[1], 16)
                    if f == 5:
                        act.wait_ge(s_sp[2], 16)
                    store_gate_a(f)
                if kind == "Y":
                    spill_ma(f)
            store_gate_b(0)
            spill_y(KC - 1)
            store_gate_b(1)

            for c in range(KC):
                act.wait_ge(s_yc, c + 1)
                if c >= 3:
                    act.wait_ge(s_ysu, c - 2)
                sq = y_sum if c == 0 else sq_y[c % 2]
                act.activation(sq[:, :], y[:, c, :], ACT.Square).then_inc(s_ysq, 1)
            for f in (2, 3):
                store_gate_b(f)
            act.wait_ge(s_var, 1)
            act.activation(ln_rs[:, :], ln_rs[:, :], ACT.Sqrt).then_inc(s_std, 1)

            def c_store(c):
                act.wait_ge(s_c, c + 1)
                if c == 0:
                    act.wait_ge(s_masp, 16 * KC)
                act.activation(c_hi[:, c, :], y[:, c, :], ACT.Copy).then_inc(s_chi, 1)

            for c in range(KC):
                act.wait_ge(s_z, c + 1)
                if c >= 2:
                    act.wait_ge(s_c, c - 1)
                act.activation(sig[c % 2][:, :], y[:, c, :], ACT.Sigmoid,
                               bias=vec[:, V_CNB + c:V_CNB + c + 1]).then_inc(s_sw, 1)
                if c:
                    c_store(c - 1)
                if c in (2, 5):
                    f = 4 if c == 2 else 5
                    store_gate_b(f)
            c_store(KC - 1)
            for f in (6, 7):
                store_gate_b(f)

            for f in range(KC):
                act.wait_ge(s_ms2, f + 1)
                act.activation(m_hi[:, f, :], gb[:, f, :], ACT.Copy).then_inc(s_mhi, 1)

            def x2_squares(t):
                act.wait_ge(s_os, 32 + 24 + t + 1)
                if t:
                    act.wait_ge(s_x2ss, t)
                row_squares(x2, t, stat[:, t:t + 1], s_x2ss, junk2)

            def x2_root(half):
                act.wait_ge(s_x2ms, half + 1)
                act.activation(stat[:, 8 + 4 * half:12 + 4 * half], stat[:, 4 * half:4 * half + 4],
                               ACT.Sqrt).then_inc(s_x2rt, 1)

            def hn_high(i):
                half, c = i // KC, i % KC
                act.wait_ge(s_x2T, i + 1)
                act.activation(hn_hi[:, c, half * HN:(half + 1) * HN], ps[:, transposed_bank(i), :], ACT.Copy,
                               scale=vec[:, V_N2 + c:V_N2 + c + 1]).then_inc(s_hnhi, 1)

            for t in range(4):
                x2_squares(t)
            x2_root(0)
            x2_squares(4)
            x2_squares(5)
            for i in range(4):
                hn_high(i)
            x2_squares(6)
            x2_squares(7)
            x2_root(1)
            for i in range(4, 2 * KC):
                hn_high(i)

            def hidden(g, par, first):
                for s in range(2):
                    act.wait_ge(s_up, 2 * g + s + 1)
                    if not first:
                        act.wait_ge(s_rsq, 2 * g + s - 1)
                    act.activation(relu_t[s][:, :], bank(2 * s, 2), ACT.Relu).then_inc(s_relu, 1)
                    if not (isinstance(g, int) and g < 2):
                        act.wait_ge(s_dn, 16 * g - 16)
                    act.wait_ge(s_rsq, 2 * g + s + 1)
                    act.activation(a_hi[par][:, s, :], relu_sq[s][:, :], ACT.Copy).then_inc(s_ahi, 1)

            hidden(0, 0, True)
            hidden(1, 1, False)
            with act.Fori(1, NFG // 2) as i:
                for par in range(2):
                    hidden(2 * i + par, par, False)

        @block.vector
        def _(dve):
            steps = 0

            def step(instruction):
                nonlocal steps
                steps += 1
                instruction.then_inc(s_dve, 1)
                dve.wait_ge(s_dve, steps)

            def mean_square(half, summed, ms):
                a, b = 4 * half, 4 * half + 4
                dve.wait_ge(summed, b)
                dve.tensor_scalar(stat[:, a:b], stat[:, a:b], 1.0 / D, EPS, ALU.mult, ALU.add).then_inc(ms, 1)

            def diagonals(half, root, done):
                a, b = 4 * half, 4 * half + 4
                dve.wait_ge(root, half + 1)
                step(dve.reciprocal(stat[:, 8 + a:8 + b], stat[:, 8 + a:8 + b]))
                for t in range(a, b):
                    dve.tensor_scalar(diag[:, t, :], ident[:, :], stat[:, 8 + t:9 + t], None, ALU.mult).then_inc(done, 1)

            def lo_part(i, dst, scale, hi, hi_sem, done):
                half, c = i // KC, i % KC
                cols = slice(half * HN, (half + 1) * HN)
                dve.wait_ge(hi_sem, i + 1)
                dve.scalar_tensor_tensor(out=dst[:, c, cols], in0=ps[:, transposed_bank(i), :], scalar=vec[:, scale + c:scale + c + 1],
                                         in1=hi[:, c, cols].bitcast(F32), op0=ALU.mult, op1=ALU.subtract).then_inc(done, 1)

            dve.wait_ge(s_ident, 6)
            mean_square(0, s_xss, s_xms)
            diagonals(0, s_xrt, s_xd)
            dve.wait_ge(s_tab, 1)
            dve.tensor_copy(vec[:, :], ps[:, 7, 0:N_VEC]).then_inc(s_tabr, 1)
            dve.tensor_copy(cw[:, :, :], ps[:, 6, 0:256].rearrange("p (c j) -> p c j", c=KC)).then_inc(s_tabr, 1)
            for i in range(KC):
                lo_part(i, h_lo, V_N1, h_hi, s_hhi, s_h)
            mean_square(1, s_xss, s_xms)
            diagonals(1, s_xrt, s_xd)
            dve.wait_ge(s_small, 16 * 5)
            step(dve.tensor_scalar(sinks_neg[:, :], sink[:, :], -1.0, None, ALU.mult))

            def qkv_sum(j):
                g, kp, t = j // 32, j // 8 % 4, j % 8
                dst, src = kv_tok[:, t, :], ps[:, t, :]
                if g < 2:
                    dst = q_tok[:, t, g * HN:(g + 1) * HN].rearrange("x (j s d) -> x s j d", j=GRP, s=2)
                    src = src.rearrange("x (s j d) -> x s j d", j=GRP, s=2)
                dve.wait_ge(s_qkvp, j + 1)
                if kp == 0:
                    dve.tensor_copy(dst, src).then_inc(s_qkvs, 1)
                else:
                    dve.wait_ge(s_qkvs, j - 7)
                    dve.tensor_tensor(dst, src, dst, ALU.add).then_inc(s_qkvs, 1)

            def head_steps(i, tok, c0, heads, gain):
                v = tok[:, :, c0:c0 + heads * HD].rearrange("p t (h d) -> p t h d", d=HD)
                rs = head_rs[:, :, 0:heads]

                def sums():
                    for th in range(2):
                        dve.wait_ge(s_sq, 2 * i + th + 1)
                        sq = squares[:, :, 0:heads * HD].rearrange("p t (h d) -> p t h d", d=HD)
                        ins = dve.tensor_reduce(head_ss[:, 4 * th:4 * th + 4, 0:heads], sq, AX.X, ALU.add)
                        ins.then_inc(s_ss, 1)
                    dve.wait_ge(s_ss, 2 * i + 2)
                    dve.tensor_scalar(head_ss[:, :, 0:heads], head_ss[:, :, 0:heads], 1.0 / HD, EPS,
                                      ALU.mult, ALU.add).then_inc(s_ms, 1)

                def norm():
                    dve.wait_ge(s_rt, i + 1)
                    step(dve.reciprocal(rs, rs))
                    for t in range(TT):
                        ins = dve.tensor_tensor(v[:, t], v[:, t], rs[:, t].unsqueeze(2).broadcast_to([P, heads, HD]), ALU.mult)
                    step(ins)

                def gains():
                    for t in range(TT):
                        ins = dve.tensor_tensor(v[:, t], v[:, t], gain[:, :].unsqueeze(1).broadcast_to([P, heads, HD]), ALU.mult)
                    step(ins)

                def rotate():
                    t1, t2 = v[:, :, :, 0:HALF], v[:, :, :, HALF:ROT]
                    cos, sin = (a[:, :, :].unsqueeze(2).broadcast_to([P, TT, heads, HALF]) for a in (cos_sb, sin_sb))
                    r = [x[:, :, 0:heads, :] for x in rope_tmp]
                    dve.tensor_tensor(r[0], t1, cos, ALU.mult)
                    dve.tensor_tensor(r[1], t2, sin, ALU.mult)
                    dve.tensor_tensor(r[2], t2, cos, ALU.mult)
                    step(dve.tensor_tensor(r[3], t1, sin, ALU.mult))
                    dve.tensor_tensor(t1, r[0], r[1], ALU.subtract)
                    dve.tensor_tensor(t2, r[2], r[3], ALU.add).then_inc(s_qk, 1)

                return [sums, norm, gains, rotate]

            q_steps = [head_steps(g, q_tok, g * HN, 8, gq) for g in range(2)]
            k_steps = head_steps(2, kv_tok, 0, N_KV, gk)
            for g in range(3):
                pieces = [[], q_steps[0], q_steps[1]][g]
                for kp in range(4):
                    for t in range(TT):
                        if g == 0 and kp == 0 and t == 4:
                            for i in range(KC, 2 * KC):
                                lo_part(i, h_lo, V_N1, h_hi, s_hhi, s_h)
                        qkv_sum(32 * g + 8 * kp + t)
                    if pieces:
                        pieces[kp]()
            for piece in k_steps:
                piece()

            def make_glu(c):
                dve.wait_ge(s_ca, c + 1)
                dve.wait_ge(s_cs, c + 1)
                g = glu_of(c)[:, PAD:PAD + S]
                dve.tensor_tensor(g, bank(bank_pair("a", c), 2), g, ALU.mult).then_inc(s_glu, 1)

            def conv_steps(c, first, last):
                g, y_c = glu_of(c), y_of(c)
                for o in range(first, min(last, CSTEPS)):
                    j, c0 = o // 2, o % 2 * HN
                    acc, src = y_c[:, c0:c0 + HN], g[:, c0 + j:c0 + j + HN]
                    if o == 0:
                        dve.wait_ge(s_glu, c + 1)
                        if c >= EARLY + 2:
                            dve.wait_ge(s_sp[c - 2], 16)
                    if j == 0:
                        ins = dve.tensor_scalar(acc, src, cw[:, c, 0:1], vec[:, V_CB + c:V_CB + c + 1], ALU.mult, ALU.add)
                    else:
                        dve.wait_ge(s_cv, CSTEPS * c + o - 1)
                        ins = dve.scalar_tensor_tensor(out=acc, in0=src, scalar=cw[:, c, j:j + 1], in1=acc,
                                                       op0=ALU.mult, op1=ALU.add)
                    ins.then_inc(s_cv, 1)

            step(dve.memset(glu_early[0][:, 0:PAD], 0.0))
            make_glu(0)

            def mask_scores(G):
                b, kv, i = G // N_KV, G % N_KV, G % 3
                lo = P if b == 0 else 0
                dve.wait_ge(s_sc, G + 1)
                if G >= 3:
                    dve.wait_ge(s_pT, G - 2)
                for j in range(GRP):
                    c0 = (j % 2) * 256
                    ins = dve.tensor_tensor_reduce(probs[i][:, j, lo:], ps[:, 4 + j // 2, c0 + lo:c0 + 256], mask[:, lo:],
                                                   HD ** -0.5, NEG, ALU.add, ALU.max, top[:, i, j:j + 1])
                step(ins)
                neg = minus_top[:, i, :]
                sinks_kv = sinks_neg[:, GRP * kv:GRP * kv + GRP]
                step(dve.scalar_tensor_tensor(out=neg, in0=top[:, i, :], scalar=-1.0, in1=sinks_kv,
                                              op0=ALU.mult, op1=ALU.min))
                dve.tensor_tensor(sink_term[:, i, :], neg, sinks_kv, ALU.subtract).then_inc(s_mx, 1)

            def invert_totals(G):
                sums = total[:, G % 3, :]
                dve.wait_ge(s_exp, G + 1)
                step(dve.tensor_tensor(sums, sums, sink_term[:, G % 3, :], ALU.add))
                dve.reciprocal(sums, sums).then_inc(s_rl, 1)

            for G in range(NG):
                for c in (1, 2):
                    if G == group_after(2 * (c - 1)):
                        dve.memset(glu_early[c][:, 0:PAD], 0.0)
                        make_glu(c)
                mask_scores(G)
                if G:
                    invert_totals(G - 1)
                else:
                    dve.wait_ge(s_v, 1)
                c = max(i for i, first in enumerate(CONV_FROM) if first <= G)
                at = SHARE * (G - CONV_FROM[c])
                conv_steps(c, at, at + SHARE)
            invert_totals(NG - 1)

            dve.wait_ge(s_pv, NG)
            step(dve.memset(glu_late[:, 0:PAD], 0.0))
            for t in range(TT):
                dve.wait_ge(s_ohi, t + 1)
                dve.tensor_tensor(o_lo[:, t, :, :], o_raw[:, t, :, :], o_hi[:, t, :, :].bitcast(F32),
                                  ALU.subtract).then_inc(s_o, 1)

            def merge_attention(f):
                dve.wait_ge(s_gas, f + 1)
                dve.wait_ge(s_ya, f + 1)
                dve.tensor_tensor(ga[:, f, :], bank(bank_pair("Y", f), 2), ga[:, f, :], ALU.mult).then_inc(s_ma, 1)

            conv_steps(EARLY - 1, SHARE * (NG - CONV_FROM[-1]), CSTEPS)
            for c in range(EARLY, KC):
                make_glu(c)
                at = MIDDLE.index(("a", c)) + 1
                after = MIDDLE[at:at + 3] if c >= 5 else []
                fs = [f for k, f in after if k == "Y"]
                for i, f in enumerate(fs):
                    conv_steps(c, 15 * i, 15 * i + 15)
                    merge_attention(f)
                conv_steps(c, 15 * len(fs), CSTEPS)

            dve.wait_ge(s_cv, CSTEPS * KC)
            for c in range(KC):
                dve.wait_ge(s_yin[c], 16)
                if c == 1:
                    ins = dve.tensor_tensor(y_sum[:, :], y[:, 0, :], y[:, 1, :], ALU.add)
                if c >= 2:
                    ins = dve.tensor_tensor(y_sum[:, :], y_sum[:, :], y[:, c, :], ALU.add)
                if 1 <= c < KC - 1:
                    step(ins)
            ins.then_inc(s_ysum, 1)
            dve.wait_ge(s_mean, 1)

            def add_squares(c):
                dve.wait_ge(s_ysq, c + 1)
                if c > 1:
                    dve.wait_ge(s_ysu, c - 1)
                dve.tensor_tensor(y_sum[:, :], y_sum[:, :], sq_y[c % 2][:, :], ALU.add).then_inc(s_ysu, 1)

            for c in range(KC):
                dve.tensor_tensor(y[:, c, :], y[:, c, :], bank(0, 2), ALU.subtract).then_inc(s_yc, 1)
                if c >= 3:
                    add_squares(c - 2)
            add_squares(KC - 2)
            add_squares(KC - 1)
            dve.wait_ge(s_vsum, 1)
            dve.tensor_scalar(ln_rs[:, :], bank(2, 2), EPS, None, ALU.add).then_inc(s_var, 1)
            dve.wait_ge(s_std, 1)
            step(dve.reciprocal(ln_rs[:, :], ln_rs[:, :]))

            def scale_row(c):
                dve.scalar_tensor_tensor(out=y[:, c, :], in0=y[:, c, :], scalar=vec[:, V_CG + c:V_CG + c + 1],
                                         in1=ln_rs[:, :], op0=ALU.mult, op1=ALU.mult).then_inc(s_z, 1)

            def c_low(c):
                dve.wait_ge(s_chi, c + 1)
                dve.tensor_tensor(c_lo[:, c, :], y[:, c, :], c_hi[:, c, :].bitcast(F32), ALU.subtract).then_inc(s_clo, 1)

            scale_row(0)
            scale_row(1)
            for c in range(KC):
                dve.wait_ge(s_sw, c + 1)
                dve.scalar_tensor_tensor(out=y[:, c, :], in0=y[:, c, :], scalar=vec[:, V_CNB + c:V_CNB + c + 1],
                                         in1=sig[c % 2][:, :], op0=ALU.add, op1=ALU.mult).then_inc(s_c, 1)
                if c + 2 < KC:
                    scale_row(c + 2)
                if c:
                    c_low(c - 1)
            c_low(KC - 1)

            for f in range(KC):
                dve.wait_ge(s_yb, f + 1)
                dve.tensor_tensor(gb[:, f, :], bank(2 * (f % 4), 2), gb[:, f, :], ALU.mult).then_inc(s_mb, 1)
                dve.wait_ge(s_mb, f + 1)
                if f == 0:
                    dve.wait_ge(s_mal, 16 * KC)
                dve.tensor_tensor(gb[:, f, :], gb[:, f, :], ma[:, f, :], ALU.add).then_inc(s_ms2, 1)
                dve.wait_ge(s_mhi, f + 1)
                dve.tensor_tensor(m_lo[:, f, :], gb[:, f, :], m_hi[:, f, :].bitcast(F32), ALU.subtract).then_inc(s_m, 1)

            for j in range(64):
                g, kp, t = j // 32, j // 8 % 4, j % TT
                dst = x2[:, t, g * HN:(g + 1) * HN]
                dve.wait_ge(s_op, j + 1)
                if g == 0 and kp == 0:
                    dve.tensor_copy(dst, ps[:, t, :]).then_inc(s_os, 1)
                    continue
                if g == 1 and kp == 0:
                    dve.tensor_tensor(dst, ps[:, t, :], xr[:, t, g * HN:(g + 1) * HN], ALU.add).then_inc(s_os, 1)
                    continue
                if g == 0 and kp == 3:
                    dve.wait_ge(s_xa, t + 1)
                else:
                    dve.wait_ge(s_os, j - 7)
                dve.tensor_tensor(dst, ps[:, t, :], dst, ALU.add).then_inc(s_os, 1)
                if j == 64 - 3:
                    mean_square(0, s_x2ss, s_x2ms)
                if j == 64 - 2:
                    diagonals(0, s_x2rt, s_x2d)
                if g == 0 and kp == 2 and t == TT - 1:
                    dve.wait_ge(s_x2in, 16 * TT)
                    for u in range(TT):
                        dst = x2[:, u, g * HN:(g + 1) * HN]
                        dve.wait_ge(s_os, j - 7 + u + 1)
                        dve.tensor_tensor(dst, dst, xr[:, u, g * HN:(g + 1) * HN], ALU.add).then_inc(s_xa, 1)
            for i in range(4):
                lo_part(i, hn_lo, V_N2, hn_hi, s_hnhi, s_hn)
            mean_square(1, s_x2ss, s_x2ms)
            diagonals(1, s_x2rt, s_x2d)
            for i in range(4, 2 * KC):
                lo_part(i, hn_lo, V_N2, hn_hi, s_hnhi, s_hn)

            def hidden(g, par, first):
                for s in range(2):
                    dve.wait_ge(s_relu, 2 * g + s + 1)
                    if not first:
                        dve.wait_ge(s_a, 2 * g + s - 1)
                    dve.tensor_tensor(relu_sq[s][:, :], relu_t[s][:, :], relu_t[s][:, :], ALU.mult).then_inc(s_rsq, 1)
                    dve.wait_ge(s_ahi, 2 * g + s + 1)
                    dve.tensor_tensor(a_lo[par][:, s, :], relu_sq[s][:, :], a_hi[par][:, s, :].bitcast(F32),
                                      ALU.subtract).then_inc(s_a, 1)

            def residual(g):
                for j in range(16):
                    s, t = j // 8, j % 8
                    dst = x2[:, t, s * HN:(s + 1) * HN]
                    dve.wait_ge(s_dn, 16 * g + j + 1)
                    if not (isinstance(g, int) and g == 0):
                        dve.wait_ge(s_ds, 16 * g + j - 15)
                    dve.tensor_tensor(dst, ps[:, 4 + t % 4, :], dst, ALU.add).then_inc(s_ds, 1)

            hidden(0, 0, True)
            hidden(1, 1, False)
            residual(0)
            with dve.Fori(0, (NFG - 2) // 2) as i:
                for par in range(2):
                    g = 2 * i + par + 1
                    hidden(g + 1, par, False)
                    residual(g)
            residual(NFG - 1)


INPUTS = ["x", "norm1_g", "w_in", "gate_b", "q_norm_g", "k_norm_g", "sinks", "w_attn_out", "conv_w", "conv_b",
          "conv_norm_g", "conv_norm_b", "w_conv_out", "w_out", "norm2_g", "w_up", "w_down"]


def kernel(**inputs):
    import concourse.bacc as bacc
    from concourse.bass_utils import run_bass_kernel_spmd

    nc = bacc.Bacc("TRN2", target_bir_lowering=False, num_devices=1)
    arrays, args = {}, []
    cos_t, sin_t = rope_tables()
    named = [(n, np.ascontiguousarray(inputs[n])) for n in INPUTS] + [("cos_t", cos_t), ("sin_t", sin_t)]
    for name, a in named:
        arrays[f"in_{name}"] = a
        args.append(nc.dram_tensor(f"in_{name}", a.shape, mybir.dt.from_np(a.dtype), kind="ExternalInput").ap())
    args.append(nc.dram_tensor("out_x", (1, S, D), F32, kind="ExternalOutput").ap())
    hybrid_block(nc, *args)
    return run_bass_kernel_spmd(nc, [arrays], core_ids=[0]).results[0]["out_x"]
```
